# Optimizing a Trainium2 kernel written in Bass

```python
import jax, jax.numpy as jnp
from jax import lax
import numpy as np

D_MODEL = 1024
BATCH = 1
SEQ = 256
DEPTH = 2

N_META = 16
CONV_WIDTH = 3
HEAD_DIM = 64
N_Q_HEADS = D_MODEL // HEAD_DIM
N_KV_HEADS = N_Q_HEADS // 4
GROUP = N_Q_HEADS // N_KV_HEADS
Q_DIM = N_Q_HEADS * HEAD_DIM
KV_DIM = N_KV_HEADS * HEAD_DIM
QKV_DIM = Q_DIM + 2 * KV_DIM
WINDOW = 128
BLOCK = 128
ROPE_THETA = 10000.0
D_FF = 7 * D_MODEL // 2
N_EXPERTS = 8
TOP_K = 2
EXPERT_FF = 7 * D_MODEL // 2
RMS_EPS = 1e-5
N_CONV_LAYERS = (DEPTH + 1) // 2
N_ATTN_LAYERS = DEPTH // 2

kernel_name = "hybrid_shortconv_swa_sink_moe_block"

def rmsnorm(x, g):
    xf = x.astype(jnp.float32)
    y = xf * lax.rsqrt(jnp.mean(xf * xf, axis=-1, keepdims=True) + RMS_EPS)
    return (y * g.astype(jnp.float32)).astype(x.dtype)

def swiglu(h, w_gate, w_up, w_down):
    return (jax.nn.silu(h @ w_gate) * (h @ w_up)) @ w_down

def short_conv_mixer(h, w_in, conv_w, w_out):
    b_gate, c_gate, u = jnp.split(h @ w_in, 3, axis=-1)
    v = c_gate * u
    L = v.shape[1]
    vp = jnp.pad(v, ((0, 0), (CONV_WIDTH - 1, 0), (0, 0)))
    conv = sum(conv_w[k] * vp[:, k:k + L] for k in range(CONV_WIDTH))
    return (b_gate * conv) @ w_out

def rope_tables(L):
    pos = jnp.arange(L, dtype=jnp.float32)
    inv = ROPE_THETA ** (-jnp.arange(0, HEAD_DIM, 2, dtype=jnp.float32) / HEAD_DIM)
    ang = pos[:, None] * inv[None, :]
    return jnp.cos(ang), jnp.sin(ang)

def apply_rope(x, cos, sin):
    x1, x2 = jnp.split(x.astype(jnp.float32), 2, axis=-1)
    c = cos[None, :, None, :]
    s = sin[None, :, None, :]
    return jnp.concatenate([x1 * c - x2 * s, x2 * c + x1 * s], axis=-1).astype(x.dtype)

def sliding_window_attention(h, w_qkv, b_qkv, sinks, w_o):
    Bsz, L, _ = h.shape
    qkv = h @ w_qkv + b_qkv
    q, k, v = jnp.split(qkv, [Q_DIM, Q_DIM + KV_DIM], axis=-1)
    q = q.reshape(Bsz, L, N_Q_HEADS, HEAD_DIM)
    k = k.reshape(Bsz, L, N_KV_HEADS, HEAD_DIM)
    v = v.reshape(Bsz, L, N_KV_HEADS, HEAD_DIM)
    cos, sin = rope_tables(L)
    q = apply_rope(q, cos, sin)
    k = apply_rope(k, cos, sin)
    pad = (-L) % BLOCK
    L_pad = L + pad
    nb = L_pad // BLOCK
    padf = lambda t: jnp.pad(t, ((0, 0), (pad, 0), (0, 0), (0, 0)))
    qb = padf(q).reshape(Bsz, nb, BLOCK, N_KV_HEADS, GROUP, HEAD_DIM)
    kb = padf(k).reshape(Bsz, nb, BLOCK, N_KV_HEADS, HEAD_DIM)
    vb = padf(v).reshape(Bsz, nb, BLOCK, N_KV_HEADS, HEAD_DIM)
    prev = lambda t: jnp.concatenate([jnp.zeros_like(t[:, :1]), t[:, :-1]], axis=1)
    kw = jnp.concatenate([prev(kb), kb], axis=2)
    vw = jnp.concatenate([prev(vb), vb], axis=2)
    scale = HEAD_DIM ** -0.5
    s = jnp.einsum('bnqhgd,bnshd->bnhgqs', qb, kw, preferred_element_type=jnp.float32) * scale
    r = jnp.arange(BLOCK)[:, None]
    j = jnp.arange(2 * BLOCK)[None, :]
    diff = BLOCK + r - j
    k_abs = jnp.arange(nb)[:, None, None] * BLOCK - BLOCK + j[None]
    mask = ((diff >= 0) & (diff < WINDOW))[None] & (k_abs >= pad)
    s = jnp.where(mask[None, :, None, None], s, -jnp.inf)
    sink = sinks.astype(jnp.float32).reshape(1, 1, N_KV_HEADS, GROUP, 1, 1)
    m = jnp.maximum(jnp.max(s, axis=-1, keepdims=True), sink)
    p = jnp.exp(s - m)
    denom = jnp.sum(p, axis=-1, keepdims=True) + jnp.exp(sink - m)
    p = (p / denom).astype(vw.dtype)
    o = jnp.einsum('bnhgqs,bnshd->bnqhgd', p, vw)
    o = o.reshape(Bsz, L_pad, Q_DIM)[:, pad:]
    return o @ w_o

def moe_swiglu(h, w_router, w_gate, w_up, w_down):
    logits = jnp.einsum('bld,de->ble', h, w_router).astype(jnp.float32)
    top_val, top_idx = lax.top_k(logits, TOP_K)
    gates = jax.nn.softmax(top_val, axis=-1)
    combine = jnp.sum(jax.nn.one_hot(top_idx, N_EXPERTS, dtype=jnp.float32) * gates[..., None], axis=-2)
    out = jnp.zeros_like(h)
    for e in range(N_EXPERTS):
        out = out + combine[..., e:e + 1].astype(h.dtype) * swiglu(h, w_gate[e], w_up[e], w_down[e])
    return out

def setup_inputs(seed: int = 0) -> dict:
    key = jax.random.key(seed)
    ks = iter(jax.random.split(key, 32))
    nrm = lambda shape, scale: jax.random.normal(next(ks), shape, jnp.float32) * scale
    gain = lambda shape: 1.0 + nrm(shape, 0.02)
    D, NA, NB = D_MODEL, N_CONV_LAYERS, N_ATTN_LAYERS
    return {
        "x": nrm((BATCH, SEQ, D), 1.0),
        "meta_tokens": nrm((N_META, D), 1.0),
        "conv_norm": gain((NA, D)),
        "conv_w_in": nrm((NA, D, 3 * D), D ** -0.5),
        "conv_w": nrm((NA, CONV_WIDTH, D), CONV_WIDTH ** -0.5),
        "conv_w_out": nrm((NA, D, D), D ** -0.5),
        "ffn_norm": gain((NA, D)),
        "ffn_w_gate": nrm((NA, D, D_FF), D ** -0.5),
        "ffn_w_up": nrm((NA, D, D_FF), D ** -0.5),
        "ffn_w_down": nrm((NA, D_FF, D), D_FF ** -0.5),
        "attn_norm": gain((NB, D)),
        "attn_w_qkv": nrm((NB, D, QKV_DIM), D ** -0.5),
        "attn_b_qkv": nrm((NB, QKV_DIM), 0.02),
        "attn_sinks": nrm((NB, N_Q_HEADS), 0.5),
        "attn_w_o": nrm((NB, Q_DIM, D), Q_DIM ** -0.5),
        "moe_norm": gain((NB, D)),
        "moe_w_router": nrm((NB, D, N_EXPERTS), D ** -0.5),
        "moe_w_gate": nrm((NB, N_EXPERTS, D, EXPERT_FF), D ** -0.5),
        "moe_w_up": nrm((NB, N_EXPERTS, D, EXPERT_FF), D ** -0.5),
        "moe_w_down": nrm((NB, N_EXPERTS, EXPERT_FF, D), EXPERT_FF ** -0.5),
        "final_norm": gain((D,)),
    }

def reference(x, meta_tokens, conv_norm, conv_w_in, conv_w, conv_w_out, ffn_norm, ffn_w_gate, ffn_w_up,
              ffn_w_down, attn_norm, attn_w_qkv, attn_b_qkv, attn_sinks, attn_w_o, moe_norm, moe_w_router,
              moe_w_gate, moe_w_up, moe_w_down, final_norm):
    Bsz = x.shape[0]
    meta = jnp.broadcast_to(meta_tokens[None].astype(x.dtype), (Bsz, N_META, D_MODEL))
    h = jnp.concatenate([meta, x], axis=1)
    for i in range(DEPTH):
        j = i // 2
        if i % 2 == 0:
            h = h + short_conv_mixer(rmsnorm(h, conv_norm[j]), conv_w_in[j], conv_w[j], conv_w_out[j])
            h = h + swiglu(rmsnorm(h, ffn_norm[j]), ffn_w_gate[j], ffn_w_up[j], ffn_w_down[j])
        else:
            h = h + sliding_window_attention(rmsnorm(h, attn_norm[j]), attn_w_qkv[j], attn_b_qkv[j],
                                             attn_sinks[j], attn_w_o[j])
            h = h + moe_swiglu(rmsnorm(h, moe_norm[j]), moe_w_router[j], moe_w_gate[j], moe_w_up[j],
                               moe_w_down[j])
    return rmsnorm(h, final_norm)[:, N_META:]


_drawn_inputs = setup_inputs


def setup_inputs(seed=0):
    import zlib

    import numpy as np

    out = dict(_drawn_inputs(seed))
    spreads = {}
    factors = {'attn_norm': 3.502, 'attn_sinks': 64.0, 'final_norm': 8.75, 'moe_norm': 4.519}
    for name, (base, spread) in spreads.items():
        noise = np.random.default_rng([zlib.crc32(name.encode()), seed]).standard_normal(out[name].shape)
        drawn = base * np.exp(spread * noise) if base else spread * noise
        out[name] = __import__('jax').numpy.asarray(drawn.astype(out[name].dtype))
    for name, factor in factors.items():
        out[name] = (out[name] * factor).astype(out[name].dtype)
    return out
```

```python
from contextlib import ExitStack

import concourse.bass as bass
from concourse import mybir

F32 = mybir.dt.float32
F32R = mybir.dt.float32r
I32 = mybir.dt.int32
ALU = mybir.AluOpType
ACT = mybir.ActivationFunctionType
AX = mybir.AxisListType.X

P = 128
D = 1024
SEQ = 256
META = 16
L = META + SEQ
DC = D // P
FF = 3584
FC = FF // P
FB = FF // 512
NE = 8
NH = 16
HD = 64
NKV = 4
WINDOW = 128
EPS = 1e-5
UNIT = 2048
HALF = UNIT // 2
SPLITS = 4
DENSE_RING = 4
RING = 7
MASKED = -1e30

N_IN, N_OUT, N_UP, N_DOWN, N_QKV, N_O = 12, 4, 28, 16, 6, 4
U_IN = 0
U_OUT = U_IN + N_IN
U_UP = U_OUT + N_OUT
U_DOWN = U_UP + N_UP
U_QKV = U_DOWN + N_DOWN
U_O = U_QKV + N_QKV
U_MOE = U_O + N_O
EXPERT_UNITS = 6 * FB
assert EXPERT_UNITS % RING == 0 and RING > DENSE_RING

CONSTS = {}
PARAMS = {}


def _columns(table, sizes):
    at = 0
    for name, n in sizes:
        table[name] = (at, n)
        at += n
    return at


N_CONSTS = _columns(CONSTS, [("ident", P), ("q_swap", P), ("k_dup0", P), ("k_dup1", P), ("k_swap0", P),
                             ("k_swap1", P), ("before", P), ("ones", P), ("iota", P), ("mask", 2 * P),
                             ("cos", L), ("sin", L), ("earlier", NE * NE), ("eps", 1)])
N_PARAMS = _columns(PARAMS, [("conv_norm", DC), ("ffn_norm", DC), ("attn_norm", DC), ("moe_norm", DC),
                             ("conv_w", 3 * DC), ("b_qkv", 12), ("sinks", NH), ("router", DC * NE),
                             ("final_norm", D)])


def expert_order():
    order = []
    for fb in range(FB):
        order += [("gate", fb, 0), ("gate", fb, 1), ("up", fb, 0), ("up", fb, 1)]
        if fb:
            order += [("down", fb - 1, 0), ("down", fb - 1, 1)]
    return order + [("down", FB - 1, 0), ("down", FB - 1, 1)]


ORDER = expert_order()
AT = {unit: n for n, unit in enumerate(ORDER)}


def moe_slot(k):
    return (k + DENSE_RING) % RING


def dense_fills(slot):
    return len(range(slot, U_MOE, DENSE_RING)) if slot < DENSE_RING else 0


def dense_place(n):
    if n < U_MOE:
        return n % DENSE_RING, n // DENSE_RING + 1
    slot = moe_slot(n - U_MOE)
    return slot, dense_fills(slot) + (n - U_MOE) // RING + 1


def trunk(nc, x_t, consts_d, params_d, conv_w_in, conv_w_out, ffn_gate, ffn_up, ffn_down, w_qkv, w_o,
          moe_gate, moe_up, moe_down, out):
    ctx = ExitStack()
    with ctx:
        def sb(name, shape, dt=F32, scope=ctx):
            return scope.enter_context(nc.sbuf_tensor(name, shape, dt))

        def sem(name):
            return ctx.enter_context(nc.semaphore(name))

        consts = sb("consts", [P, N_CONSTS])
        params = sb("params", [P, N_PARAMS])
        h = sb("h", [P, DC, L])
        raw = sb("raw", [P, RING, UNIT])
        hi = sb("hi", [P, SPLITS, HALF], F32R)
        lo = sb("lo", [P, SPLITS, HALF], F32R)

        def const(name):
            at, n = CONSTS[name]
            return consts[:, at:at + n]

        def param(name, a=0, n=None):
            at, size = PARAMS[name]
            return params[:, at + a:at + (size if n is None else a + n)]

        ident = const("ident")

        with ExitStack() as dense:
            xn = sb("xn", [P, DC, L], scope=dense)
            xh = sb("xh", [P, DC, L], F32R, dense)
            xl = sb("xl", [P, DC, L], F32R, dense)
            rstd = sb("rstd", [P, L], scope=dense)
            with ExitStack() as s:
                u_act = sb("u_act", [P, DC, L], scope=s)
                v_act = sb("v_act", [P, DC, L + 2], scope=s)
                conv = sb("conv", [P, DC, L], scope=s)
                yh = sb("yh", [P, DC, L], F32R, s)
                yl = sb("yl", [P, DC, L], F32R, s)
            with ExitStack() as s:
                hid_h = sb("hid_h", [P, FC, L], F32R, s)
                hid_l = sb("hid_l", [P, FC, L], F32R, s)
                gate_act = sb("gate_act", [P, 2, L], scope=s)
                hid = sb("hid", [P, 2, L], scope=s)
            with ExitStack() as s:
                q_t = sb("q_t", [P, DC, SEQ], scope=s)
                q_rot = sb("q_rot", [P, DC, SEQ], scope=s)
                kv_t = sb("kv_t", [P, 4, L], scope=s)
                k_rot = sb("k_rot", [P, NKV, 2, L], scope=s)
                rope_a = sb("rope_a", [P, 2, L], scope=s)
                rope_b = sb("rope_b", [P, 2, L], scope=s)
                v_meta = sb("v_meta", [META, 4 * HD], scope=s)
                v_tok = sb("v_tok", [P, 2, 4 * HD], scope=s)
                prob = sb("prob", [P, 2, 2, SEQ], scope=s)
                prob_t = sb("prob_t", [P, 2, 4, P], scope=s)
                neg_max = sb("neg_max", [P, 2, NH], scope=s)
                neg_sink = sb("neg_sink", [P, NH], scope=s)
                row_max = sb("row_max", [P, 2], scope=s)
                prob_sum = sb("prob_sum", [P, 2, NH], scope=s)
                sink_exp = sb("sink_exp", [P, 2, NH], scope=s)
                o_tok = sb("o_tok", [P, 2, D], scope=s)
                oh = sb("oh", [P, DC, SEQ], F32R, s)
                ol = sb("ol", [P, DC, SEQ], F32R, s)

        with ExitStack() as moe:
            y = sb("y", [P, NE, D], scope=moe)
            xt_h = sb("xt_h", [P, 2, D], F32R, moe)
            xt_l = sb("xt_l", [P, 2, D], F32R, moe)
            acc = sb("acc", [P, 2, D], scope=moe)
            pick = sb("pick", [P, 2, NE + 1, P], F32R, moe)
            place = sb("place", [P, NE, SEQ], scope=moe)
            xe_h = sb("xe_h", [P, DC, P], F32R, moe)
            xe_l = sb("xe_l", [P, DC, P], F32R, moe)
            ht_h = sb("ht_h", [P, 2, 4, P], F32R, moe)
            ht_l = sb("ht_l", [P, 2, 4, P], F32R, moe)
            logit = sb("logit", [P, 2, NE], scope=moe)
            pair_a = sb("pair_a", [P, 2, NE, NE], scope=moe)
            pair_b = sb("pair_b", [P, 2, NE, NE], scope=moe)
            rank = sb("rank", [P, 2, NE], scope=moe)
            chosen = sb("chosen", [P, 2, NE], scope=moe)
            chosen_sum = sb("chosen_sum", [P, NE], scope=moe)
            combine = sb("combine", [P, 2, NE], scope=moe)
            top = sb("top", [P, 2], scope=moe)
            gate_sum = sb("gate_sum", [P, 2], scope=moe)
            slot_of = sb("slot_of", [P, 2, NE], scope=moe)
            most = sb("most", [P, 1], scope=moe)
            most_i = sb("most_i", [P, 1], I32, moe)
            sq_sum = sb("sq_sum", [P, 2], scope=moe)
            final_std = sb("final_std", [P, 2], scope=moe)
            final_rstd = sb("final_rstd", [P, 2], scope=moe)
            with ExitStack() as s:
                placed = sb("placed", [P, 2, NE, P], scope=s)
            with ExitStack() as s:
                silu_g = sb("silu_g", [P, 2, 512], scope=s)
                hid_e = sb("hid_e", [P, 2, 512], scope=s)

        bank = [ctx.enter_context(nc.psum_tensor(f"bank{i}", [P, 512], F32)) for i in range(8)]

        s_stream = sem("stream_landed")
        s_raw = [sem(f"raw_landed{i}") for i in range(RING)]
        s_hi = sem("hi_ready")
        s_lo = sem("lo_ready")
        s_used = sem("half_used")
        s_sq = sem("squares_ready")
        s_ss = sem("square_sums_ready")
        s_std = sem("std_ready")
        s_xn = sem("xn_ready")
        s_xh = sem("xh_ready")
        s_xl = sem("xl_ready")
        s_tile_dve = sem("tiles_read_by_dve")
        s_tile_act = sem("tiles_read_by_act")
        s_yh = sem("yh_ready")
        s_yl = sem("yl_ready")
        s_hid = sem("hid_ready")
        s_hidh = sem("hid_h_ready")
        s_hidl = sem("hid_l_ready")
        s_rope = sem("rope_products")
        s_rope_read = sem("rope_read")
        s_rot = sem("rotated")
        s_v = sem("v_turned")
        s_v_sb = sem("v_ready")
        s_score = sem("scores_ready")
        s_masked = sem("scores_masked")
        s_negmax = sem("neg_max_ready")
        s_exp = sem("prob_ready")
        s_pt = sem("prob_turned")
        s_pt_sb = sem("prob_t_ready")
        s_pv = sem("values_summed")
        s_sink = sem("sink_shifted")
        s_sink_exp = sem("sink_exp_ready")
        s_o = sem("o_ready")
        s_ot = sem("o_turned")
        s_oh = sem("oh_ready")
        s_ol = sem("ol_ready")
        s_h_turned = sem("h_turned")
        s_acc = sem("acc_ready")
        s_xt = sem("xn_turned")
        s_xth = sem("xt_h_ready")
        s_xtl = sem("xt_l_ready")
        s_logit = sem("logits_ready")
        s_top = sem("top_ready")
        s_gexp = sem("gate_exp_ready")
        s_chosen = sem("chosen_ready")
        s_pos = sem("positions_ready")
        s_slot = sem("slot_of_ready")
        s_comb = sem("combine_ready")
        s_pick = sem("pick_ready")
        s_placed = sem("placed_ready")
        s_place_t = sem("place_turned")
        s_place = sem("place_ready")
        s_gath = sem("tokens_gathered")
        s_xe = sem("xe_ready")
        s_silu = sem("silu_ready")
        s_mult = sem("hidden_ready")
        s_ht = sem("hidden_turned")
        s_hth = sem("ht_h_ready")
        s_htl = sem("ht_l_ready")
        s_yfree = sem("y_banks_read")
        s_comb_done = sem("experts_summed")
        s_most = sem("most_ready")
        s_accs = sem("acc_summed")
        s_done = sem("moe_done")
        s_fsq = sem("final_squares_ready")
        s_fstd = sem("final_std_ready")
        s_out = sem("out_ready")
        s_stored = sem("out_stored")
        s_link = sem("dve_chain")

        w_in = conv_w_in.rearrange("(c p) n -> p c n", p=P)
        w_out = conv_w_out.rearrange("(c p) n -> p c n", p=P)
        w_fg = ffn_gate.rearrange("(c p) n -> p c n", p=P)
        w_fu = ffn_up.rearrange("(c p) n -> p c n", p=P)
        w_fd = ffn_down.rearrange("(m c p) n -> p m c n", p=P, c=7)
        w_qkv_v = w_qkv.rearrange("(c p) n -> p c n", p=P)
        w_o_v = w_o.rearrange("(c p) n -> p c n", p=P)
        out_v = out.rearrange("a (t p) d -> p (a t) d", p=P)

        def load_expert_unit(sp, e, u, wait):
            kind, fb, part = ORDER[u]
            slot = moe_slot(u)
            if wait is not None:
                if isinstance(wait, int) and wait < RING:
                    before = max(n for n in range(U_MOE) if n % DENSE_RING == slot)
                    sp.wait_ge(s_lo, 2 * before + 2)
                else:
                    sp.wait_ge(s_lo, 2 * (U_MOE + wait - RING) + 2)
            if kind == "down":
                src = moe_down[bass.ds(e * FF + 512 * fb + 256 * part, 256), :].rearrange("(c p) n -> p c n", p=P)
                dst = raw[:, slot, :].rearrange("p (c n) -> p c n", n=D)
            else:
                w = moe_gate if kind == "gate" else moe_up
                src = w[bass.ds(e * D + 512 * part, 512), 512 * fb:512 * (fb + 1)].rearrange(
                    "(c p) n -> p c n", p=P)
                dst = raw[:, slot, :].rearrange("p (c n) -> p c n", n=512)
            sp.dma_start(dst, src).then_inc(s_raw[slot], 16)

        def overflow(eng, body):
            eng.wait_ge(s_most, 1)
            count = eng.value_load(most_i[0:1, 0:1], min_val=0, max_val=SEQ)
            with eng.If(count > P):
                body()

        block = ctx.enter_context(nc.Block())

        @block.sync
        def _(sp):
            sp.dma_start(h[:], x_t.rearrange("(c p) t -> p c t", p=P)).then_inc(s_stream, 16)
            sp.dma_start(consts[:], consts_d).then_inc(s_stream, 16)
            sp.dma_start(params[:], params_d).then_inc(s_stream, 16)

            def load(n, slot, src, wait=True, size=UNIT):
                if wait:
                    sp.wait_ge(s_lo, 2 * n - 2 * DENSE_RING + 2)
                dst = raw[:, slot, 0:size].rearrange("p (c n) -> p c n", n=256)
                sp.dma_start(dst, src).then_inc(s_raw[slot], 16)

            for m in range(N_IN):
                at = D * (2 - m // 4) + 256 * (m % 4)
                load(U_IN + m, m % 4, w_in[:, :, at:at + 256], wait=m >= DENSE_RING)
            for k in range(RING - DENSE_RING):
                load_expert_unit(sp, 0, k, wait=None)
            for s in range(4):
                load(U_OUT + s, s, w_out[:, :, 256 * s:256 * (s + 1)])
            with sp.Fori(0, 7) as i:
                for s in range(4):
                    w = (w_fg, w_fu)[s % 2]
                    load(U_UP + 4 * i + s, s, w[:, :, bass.ds(512 * i + 256 * (s // 2), 256)])
            with sp.Fori(0, 4) as q:
                for s in range(4):
                    load(U_DOWN + 4 * q + s, s, w_fd[:, s, :, bass.ds(256 * q, 256)], size=7 * 256)
            for m in range(N_QKV):
                at = D + 256 * m if m < 2 else 256 * (m - 2)
                load(U_QKV + m, (U_QKV + m) % 4, w_qkv_v[:, :, at:at + 256])
            for m in range(N_O):
                load(U_O + m, (U_O + m) % 4, w_o_v[:, :, 256 * m:256 * (m + 1)])

            def experts(r):
                first = RING - DENSE_RING if r == 0 else 2
                for u in range(first, EXPERT_UNITS):
                    load_expert_unit(sp, 0, u, wait=r * NE * EXPERT_UNITS + u)
                with sp.Fori(1, NE) as e:
                    for u in range(EXPERT_UNITS):
                        load_expert_unit(sp, e, u, wait=(r * NE + e) * EXPERT_UNITS + u)
                for u in range(2):
                    load_expert_unit(sp, 0, u, wait=(r + 1) * NE * EXPERT_UNITS + u)

            experts(0)
            overflow(sp, lambda: experts(1))
            for t in range(2):
                sp.wait_ge(s_out, t + 1)
                sp.dma_start(out_v[:, t, :], acc[:, t, :]).then_inc(s_stored, 16)
            sp.wait_ge(s_stored, 32)

        @block.scalar
        def _(act):
            def split_hi(n, slot, parity, fill):
                act.wait_ge(s_raw[slot], 16 * fill)
                for x in range(2):
                    if not (isinstance(n, int) and 2 * n + x < SPLITS):
                        act.wait_ge(s_used, 2 * n + x - SPLITS + 1)
                    nc.scalar.copy(hi[:, 2 * parity + x, :],
                                   raw[:, slot, HALF * x:HALF * (x + 1)]).then_inc(s_hi, 1)

            def dense_hi(n):
                slot, fill = dense_place(n)
                split_hi(n, slot, n % 2, fill)

            def norm(k, t0, ready, ready_at, with_split):
                act.wait_ge(ready, ready_at)
                nc.scalar.activation(xn[:, :, t0:L], h[:, :, t0:L], ACT.Square).then_inc(s_sq, 1)
                if k == 0:
                    dense_hi(0)
                    dense_hi(1)
                act.wait_ge(s_ss, k + 1)
                nc.scalar.activation(rstd[:, t0:L], bank[7][:, 0:L - t0], ACT.Sqrt, bias=eps_col,
                                     scale=1.0 / D).then_inc(s_std, 1)
                if with_split:
                    for c in range(DC):
                        act.wait_ge(s_xn, DC * k + c + 1)
                        nc.scalar.copy(xh[:, c, :], xn[:, c, :]).then_inc(s_xh, 1)

            eps_col = const("eps")
            act.sem_inc(s_tile_act, 4)
            act.sem_inc(s_silu, 2)
            act.sem_inc(s_yfree, 2)
            norm(0, 0, s_stream, 48, True)

            for m in range(N_IN):
                n = U_IN + m
                if m >= 8:
                    for j in range(2):
                        blk = 2 * (m - 8) + j
                        act.wait_ge(s_tile_dve, 8 + 16 + blk + 1)
                        nc.scalar.copy(yh[:, blk, :], conv[:, blk, :]).then_inc(s_yh, 1)
                dense_hi(n + 2)
            for m in range(N_OUT):
                dense_hi(U_OUT + m + 2)
            norm(1, 0, s_tile_dve, 40, True)

            with act.Fori(0, 7) as i:
                for par in range(2):
                    p = 2 * i + par
                    gate_unit = U_UP + 4 * i + 2 * par
                    act.wait_ge(s_used, 2 * gate_unit + 2)
                    for j in range(2):
                        act.wait_ge(s_hid, 2 * p + j + 3)
                        nc.scalar.activation(gate_act[:, j, :], bank[4 * par + j][:, 0:L],
                                             ACT.Silu).then_inc(s_tile_act, 1)
                    for k in (2, 3):
                        ph = 2 * par + k
                        split_hi(gate_unit + k, ph % 4, ph % 2, U_UP // 4 + i + 1 + ph // 4)
                    for j in range(2):
                        act.wait_ge(s_hid, 4 + 2 * p + j + 1)
                        nc.scalar.copy(hid_h[:, bass.ds(2 * p + j, 1), :], hid[:, j:j + 1, :]).then_inc(s_hidh, 1)
            for m in range(N_DOWN):
                dense_hi(U_DOWN + m + 2)
            norm(2, 0, s_tile_dve, 48, True)

            for m in range(N_QKV):
                n = U_QKV + m
                act.wait_ge(s_used, 2 * n + 2)
                for j in range(2):
                    tile = 2 * m + j
                    src = bank[tile % 8]
                    if m < 2:
                        nc.scalar.activation(kv_t[:, tile, :], src[:, 0:L], ACT.Identity,
                                             bias=param("b_qkv", 8 + tile, 1)).then_inc(s_tile_act, 1)
                    else:
                        b = tile - 4
                        nc.scalar.activation(q_t[:, b, :], src[:, 0:SEQ], ACT.Identity,
                                             bias=param("b_qkv", b, 1)).then_inc(s_tile_act, 1)
                dense_hi(n + 2)
            act.wait_ge(s_v, 2)
            nc.scalar.copy(v_meta[:], bank[0][0:META, 0:256]).then_inc(s_v_sb, 1)
            nc.scalar.copy(v_tok[:].rearrange("p t n -> p (t n)"), bank[1][:, 0:512]).then_inc(s_v_sb, 1)

            def turned_probs(s):
                act.wait_ge(s_pt, s + 1)
                if s >= 2:
                    act.wait_ge(s_pv, s - 1)
                src = bank[4 + s % 2][:].rearrange("p (i k q) -> p i k q", i=2, k=2)
                dst = prob_t[:, s % 2].rearrange("p (i k) q -> p i k q", i=2)
                if s < 8:
                    nc.scalar.copy(dst[0:META, :, 0, :], src[0:META, :, 0, :]).then_inc(s_pt_sb, 1)
                    nc.scalar.copy(dst[:, :, 1, :], src[:, :, 1, :]).then_inc(s_pt_sb, 1)
                else:
                    nc.scalar.copy(dst, src).then_inc(s_pt_sb, 2)

            for s in range(16):
                t, b = s // 8, s % 8
                k0 = P - META if t == 0 else 0
                act.wait_ge(s_negmax, s + 1)
                for i in range(2):
                    nc.scalar.activation(prob[:, s % 2, i, k0:], prob[:, s % 2, i, k0:], ACT.Exp,
                                         bias=neg_max[:, t, 2 * b + i:2 * b + i + 1],
                                         accum_out=prob_sum[:, t, 2 * b + i:2 * b + i + 1]).then_inc(s_exp, 1)
                if s:
                    turned_probs(s - 1)
            turned_probs(15)
            act.wait_ge(s_sink, 1)
            nc.scalar.activation(sink_exp[:].rearrange("p t n -> p (t n)"),
                                 sink_exp[:].rearrange("p t n -> p (t n)"), ACT.Exp).then_inc(s_sink_exp, 1)
            for g in range(4):
                t, q = g // 2, g % 2
                act.wait_ge(s_ot, g + 1)
                nc.scalar.copy(oh[:, 4 * q:4 * q + 4, P * t:P * (t + 1)],
                               bank[(6, 7, 0, 1)[g]][:].rearrange("p (c n) -> p c n", c=4)).then_inc(s_oh, 1)
            for m in range(N_O):
                dense_hi(U_O + m + 2)

            norm(3, META, s_tile_dve, 56, False)
            for g in range(4):
                act.wait_ge(s_h_turned, g + 1)
                nc.scalar.copy(acc[:, g // 2, 512 * (g % 2):512 * (g % 2 + 1)], bank[3 + g][:]).then_inc(s_acc, 1)
            for g in range(4):
                act.wait_ge(s_xt, g + 1)
                nc.scalar.copy(xt_h[:, g // 2, 512 * (g % 2):512 * (g % 2 + 1)],
                               bank[(0, 1, 2, 7)[g]][:]).then_inc(s_xth, 1)
            for t in range(2):
                act.wait_ge(s_top, 1)
                nc.scalar.activation(combine[:, t, :], logit[:, t, :], ACT.Exp,
                                     bias=top[:, t:t + 1]).then_inc(s_gexp, 1)

            def turned_hi(e, fb):
                act.wait_ge(s_ht, FB * e + fb + 1)
                nc.scalar.copy(ht_h[:, fb % 2], bank[4][:].rearrange("p (c n) -> p c n", c=4)).then_inc(s_hth, 1)

            def gathered_hi(count, g):
                act.wait_ge(s_gath, count + g + 1)
                nc.scalar.copy(xe_h[:, 4 * g:4 * g + 4, :],
                               bank[5][:].rearrange("p (c n) -> p c n", c=4)).then_inc(s_xe, 1)

            def experts(r):
                for g in range(4):
                    t, q = g // 2, g % 2
                    act.wait_ge(s_place_t, 4 * r + g + 1)
                    ins = nc.scalar.copy(place[:, 4 * q:4 * q + 4, P * t:P * (t + 1)],
                                         bank[g][:].rearrange("p (c n) -> p c n", c=4))
                    ins.then_inc(s_place, 1)
                for g in range(2):
                    gathered_hi(4 * (NE + 1) * r, g)
                with act.Fori(0, NE) as el:
                    e = el + NE * r
                    for u, (kind, fb, part) in enumerate(ORDER):
                        n = U_MOE + EXPERT_UNITS * e + u
                        if (kind, part) == ("gate", 1):
                            act.wait_ge(s_used, 2 * n + 2)
                            act.wait_ge(s_mult, FB * e + fb + (1 if fb else 2))
                            nc.scalar.activation(silu_g[:, fb % 2, :], bank[fb % 2][:], ACT.Silu).then_inc(s_silu, 1)
                        if (kind, fb, part) == ("down", FB - 1, 1):
                            act.wait_ge(s_used, 2 * n + 2)
                            nc.scalar.copy(y[:, bass.ds(el, 1), 0:512],
                                           bank[6][:].rearrange("p (a n) -> p a n", a=1)).then_inc(s_yfree, 1)
                        slot = moe_slot((u + 2) % EXPERT_UNITS)
                        fill = dense_fills(slot) + (EXPERT_UNITS // RING) * e + (u + 2) // RING + 1
                        split_hi(n + 2, slot, u % 2, fill)
                        if (kind, part) == ("gate", 1) and fb:
                            turned_hi(e, fb - 1)
                        if (kind, fb, part) == ("up", FB - 1, 1):
                            gathered_hi(4 * (e + 1) + 4 * r, 0)
                        if (kind, fb, part) == ("down", FB - 2, 0):
                            gathered_hi(4 * (e + 1) + 4 * r, 1)
                        if (kind, fb, part) == ("down", FB - 2, 1):
                            turned_hi(e, FB - 1)

            experts(0)
            overflow(act, lambda: experts(1))
            act.wait_ge(s_done, 1)
            for t in range(2):
                nc.scalar.activation(y[:, t, :], acc[:, t, :], ACT.Square,
                                     accum_out=sq_sum[:, t:t + 1]).then_inc(s_fsq, 1)
            act.wait_ge(s_fsq, 2)
            nc.scalar.activation(final_std[:], sq_sum[:], ACT.Sqrt, bias=eps_col, scale=1.0 / D).then_inc(s_fstd, 1)

        @block.vector
        def _(dve):
            v = nc.vector
            links = [0]

            def link(ins):
                links[0] += 1
                ins.then_inc(s_link, 1)
                dve.wait_ge(s_link, links[0])

            def split_lo(n, slot, parity):
                for x in range(2):
                    dve.wait_ge(s_hi, 2 * n + x + 1)
                    at = 2 * parity + x
                    v.tensor_tensor(lo[:, at, :], raw[:, slot, HALF * x:HALF * (x + 1)], hi[:, at, :].bitcast(F32),
                                    ALU.subtract).then_inc(s_lo, 1)

            def dense_lo(n):
                split_lo(n, dense_place(n)[0], n % 2)

            def norm(k, t0, name, with_split):
                if k == 0:
                    dense_lo(0)
                    dense_lo(1)
                dve.wait_ge(s_std, k + 1)
                link(v.reciprocal(rstd[:, t0:L], rstd[:, t0:L]))

                def low(c):
                    dve.wait_ge(s_xh, DC * k + c + 1)
                    v.tensor_tensor(xl[:, c, :], xn[:, c, :], xh[:, c, :].bitcast(F32), ALU.subtract).then_inc(s_xl, 1)

                for c in range(DC):
                    v.scalar_tensor_tensor(out=xn[:, c, t0:L], in0=h[:, c, t0:L], scalar=param(name, c, 1),
                                           in1=rstd[:, t0:L], op0=ALU.mult, op1=ALU.mult).then_inc(s_xn, 1)
                    if with_split and c:
                        low(c - 1)
                if with_split:
                    low(DC - 1)

            dve.sem_inc(s_hid, 4)
            dve.sem_inc(s_hidl, 2)
            dve.sem_inc(s_mult, 2)
            dve.sem_inc(s_htl, 1)
            v.memset(v_act[:, :, 0:2], 0.0).then_inc(s_tile_dve, 8)
            norm(0, 0, "conv_norm", True)

            for m in range(N_IN):
                n = U_IN + m
                dve.wait_ge(s_used, 2 * n + 2)
                for j in range(2):
                    tile = 2 * m + j
                    blk = tile % 8
                    src = bank[blk][:, 0:L]
                    if m < 4:
                        v.tensor_copy(u_act[:, blk, :], src).then_inc(s_tile_dve, 1)
                    elif m < 8:
                        v.tensor_tensor(v_act[:, blk, 2:], src, u_act[:, blk, :], ALU.mult).then_inc(s_tile_dve, 1)
                    else:
                        v.tensor_tensor(conv[:, blk, :], src, conv[:, blk, :], ALU.mult).then_inc(s_tile_dve, 1)
                dense_lo(n + 2)
                for j in range(2):
                    tile = 2 * m + j
                    blk = tile % 8
                    if 4 <= m < 8:
                        dve.wait_ge(s_tile_dve, 8 + tile + 1)
                        link(v.tensor_scalar(conv[:, blk, :], v_act[:, blk, 0:L], param("conv_w", blk, 1), None,
                                             ALU.mult))
                        for k in (1, 2):
                            link(v.scalar_tensor_tensor(out=conv[:, blk, :], in0=v_act[:, blk, k:k + L],
                                                        scalar=param("conv_w", DC * k + blk, 1),
                                                        in1=conv[:, blk, :], op0=ALU.mult, op1=ALU.add))
                    elif m >= 8:
                        dve.wait_ge(s_yh, blk + 1)
                        v.tensor_tensor(yl[:, blk, :], conv[:, blk, :], yh[:, blk, :].bitcast(F32),
                                        ALU.subtract).then_inc(s_yl, 1)

            def add_tile(tile, src, t0):
                v.tensor_tensor(h[:, tile, t0:L], h[:, tile, t0:L], src[:, 0:L - t0], ALU.add).then_inc(s_tile_dve, 1)

            for m in range(N_OUT):
                dve.wait_ge(s_used, 2 * (U_OUT + m) + 2)
                for j in range(2):
                    add_tile(2 * m + j, bank[2 * m + j], 0)
                dense_lo(U_OUT + m + 2)
            norm(1, 0, "ffn_norm", True)

            with dve.Fori(0, 7) as i:
                for par in range(2):
                    p = 2 * i + par
                    gate_unit = U_UP + 4 * i + 2 * par
                    split_lo(gate_unit + 2, (2 * par + 2) % 4, 0)
                    dve.wait_ge(s_used, 2 * gate_unit + 4)
                    for j in range(2):
                        dve.wait_ge(s_tile_act, 4 + 2 * p + j + 1)
                        dve.wait_ge(s_hidl, 2 * p + j + 1)
                        v.tensor_tensor(hid[:, j, :], bank[4 * par + 2 + j][:, 0:L], gate_act[:, j, :],
                                        ALU.mult).then_inc(s_hid, 1)
                    split_lo(gate_unit + 3, (2 * par + 3) % 4, 1)
                    for j in range(2):
                        dve.wait_ge(s_hidh, 2 * p + j + 1)
                        f = bass.ds(2 * p + j, 1)
                        v.tensor_tensor(hid_l[:, f, :], hid[:, j:j + 1, :], hid_h[:, f, :].bitcast(F32),
                                        ALU.subtract).then_inc(s_hidl, 1)

            for m in range(N_DOWN):
                if m % 4 == 3:
                    q = m // 4
                    dve.wait_ge(s_used, 2 * (U_DOWN + m) + 2)
                    for j in range(2):
                        add_tile(2 * q + j, bank[2 * (q % 2) + j], 0)
                dense_lo(U_DOWN + m + 2)
            norm(2, 0, "attn_norm", True)

            for m in range(N_QKV):
                dense_lo(U_QKV + m + 2)
            link(v.memset(k_rot[:], 0.0))
            link(v.tensor_scalar(neg_sink[:], param("sinks"), -1.0, None, ALU.mult))
            cos, sin = const("cos"), const("sin")
            for g in range(NKV):
                if g >= 2:
                    dve.wait_ge(s_rot, 2 * g - 2)
                dve.wait_ge(s_rope, 2 * g + 1)
                v.tensor_tensor(rope_a[:, g % 2, :], bank[2 * g][:, 0:L], cos, ALU.mult).then_inc(s_rope_read, 1)
                dve.wait_ge(s_rope, 2 * g + 2)
                v.tensor_tensor(rope_b[:, g % 2, :], bank[2 * g + 1][:, 0:L], sin, ALU.mult).then_inc(s_rope_read, 1)
                dve.wait_ge(s_rope_read, 2 * g + 2)
                for i in range(2):
                    half = slice(HD * i, HD * (i + 1))
                    ins = v.tensor_tensor(k_rot[half, g, i, :], rope_a[half, g % 2, :], rope_b[half, g % 2, :],
                                          ALU.add)
                    ins.then_inc(s_rot, 1)
            dve.wait_ge(s_tile_act, 44)
            for b in range(DC):
                dve.wait_ge(s_rot, 6 + 2 * b if b < 2 else 8 + b - 1)
                link(v.tensor_tensor(rope_a[:, b % 2, 0:SEQ], q_t[:, b, :], cos[:, META:L], ALU.mult))
                dve.wait_ge(s_rope, 8 + b + 1)
                v.tensor_tensor(rope_b[:, b % 2, 0:SEQ], bank[b][:, 0:SEQ], sin[:, META:L],
                                ALU.mult).then_inc(s_rope_read, 1)
                dve.wait_ge(s_rope_read, 8 + b + 1)
                v.tensor_tensor(q_rot[:, b, :], rope_a[:, b % 2, 0:SEQ], rope_b[:, b % 2, 0:SEQ],
                                ALU.add).then_inc(s_rot, 1)

            for s in range(16):
                t, b = s // 8, s % 8
                k0 = P - META if t == 0 else 0
                width = 2 * P - k0
                dve.wait_ge(s_score, s + 1)
                if s >= 2:
                    dve.wait_ge(s_pt, s - 1)
                part = prob[:, s % 2, :, k0:]
                mask = const("mask")[:, k0:].unsqueeze(1).to_broadcast([P, 2, width])
                scores = bank[2 + s % 2][:].rearrange("p (i k) -> p i k", i=2)[:, :, k0:]
                v.scalar_tensor_tensor(out=part, in0=scores, scalar=HD ** -0.5, in1=mask, op0=ALU.mult,
                                       op1=ALU.add).then_inc(s_masked, 1)
                dve.wait_ge(s_masked, s + 1)
                if s:
                    dve.wait_ge(s_negmax, s)
                link(v.tensor_reduce(row_max[:], part, AX, ALU.max))
                v.scalar_tensor_tensor(out=neg_max[:, t, 2 * b:2 * b + 2], in0=row_max[:], scalar=-1.0,
                                       in1=neg_sink[:, 2 * b:2 * b + 2], op0=ALU.mult,
                                       op1=ALU.min).then_inc(s_negmax, 1)
            dve.wait_ge(s_negmax, 16)
            v.tensor_tensor(sink_exp[:], neg_max[:], param("sinks").unsqueeze(1).to_broadcast([P, 2, NH]),
                            ALU.add).then_inc(s_sink, 1)
            dve.wait_ge(s_exp, 32)
            dve.wait_ge(s_sink_exp, 1)
            link(v.tensor_tensor(sink_exp[:], sink_exp[:], prob_sum[:], ALU.add))
            link(v.reciprocal(sink_exp[:], sink_exp[:]))
            for g in range(4):
                t, q = g // 2, g % 2
                dve.wait_ge(s_pv, 8 * (t + 1))
                v.tensor_tensor(o_tok[:, t, 512 * q:512 * (q + 1)].rearrange("p (n d) -> p n d", d=HD),
                                bank[(6, 7, 0, 1)[g]][:].rearrange("p (n d) -> p n d", d=HD),
                                sink_exp[:, t, 8 * q:8 * q + 8].unsqueeze(2).to_broadcast([P, 8, HD]),
                                ALU.mult).then_inc(s_o, 1)
            for g in range(4):
                t, q = g // 2, g % 2
                dve.wait_ge(s_oh, g + 1)
                dst = (slice(None), slice(4 * q, 4 * q + 4), slice(P * t, P * (t + 1)))
                v.tensor_tensor(ol[dst], bank[(6, 7, 0, 1)[g]][:].rearrange("p (c n) -> p c n", c=4),
                                oh[dst].bitcast(F32), ALU.subtract).then_inc(s_ol, 1)
            for m in range(N_O):
                dve.wait_ge(s_used, 2 * (U_O + m) + 2)
                for j in range(2):
                    add_tile(2 * m + j, bank[2 * m + j], META)
                dense_lo(U_O + m + 2)
            norm(3, META, "moe_norm", False)

            for g in range(4):
                dve.wait_ge(s_xth, g + 1)
                dst = (slice(None), g // 2, slice(512 * (g % 2), 512 * (g % 2 + 1)))
                v.tensor_tensor(xt_l[dst], bank[(0, 1, 2, 7)[g]][:], xt_h[dst].bitcast(F32),
                                ALU.subtract).then_inc(s_xtl, 1)

            dve.wait_ge(s_logit, 1)
            link(v.tensor_copy(logit[:].rearrange("p t n -> p (t n)"), bank[3][:, 0:2 * NE]))
            link(v.tensor_reduce(top[:], logit[:], AX, ALU.max))
            v.tensor_scalar(top[:], top[:], -1.0, None, ALU.mult).then_inc(s_top, 1)
            for t in range(2):
                other = logit[:, t, :].unsqueeze(1).to_broadcast([P, NE, NE])
                own = logit[:, t, :].unsqueeze(2).to_broadcast([P, NE, NE])
                earlier = const("earlier").rearrange("p (a b) -> p a b", a=NE)
                link(v.tensor_tensor(pair_a[:, t], other, own, ALU.is_gt))
                link(v.tensor_tensor(pair_b[:, t], other, own, ALU.is_equal))
                link(v.tensor_tensor(pair_b[:, t], pair_b[:, t], earlier, ALU.mult))
                link(v.tensor_tensor(pair_a[:, t], pair_a[:, t], pair_b[:, t], ALU.add))
                link(v.tensor_reduce(rank[:, t], pair_a[:, t], AX, ALU.add))
            link(v.tensor_scalar(chosen[:], rank[:], 1.5, None, ALU.is_lt))
            v.tensor_tensor(chosen_sum[:], chosen[:, 0], chosen[:, 1], ALU.add).then_inc(s_chosen, 1)
            dve.wait_ge(s_gexp, 2)
            link(v.tensor_tensor(combine[:], combine[:], chosen[:], ALU.mult))
            link(v.tensor_reduce(gate_sum[:], combine[:], AX, ALU.add))
            link(v.reciprocal(gate_sum[:], gate_sum[:]))
            v.tensor_tensor(combine[:], combine[:], gate_sum[:].unsqueeze(2).to_broadcast([P, 2, NE]),
                            ALU.mult).then_inc(s_comb, 1)
            dve.wait_ge(s_pos, 1)
            v.tensor_copy(slot_of[:].rearrange("p t n -> p (t n)"), bank[4][:, 0:2 * NE]).then_inc(s_slot, 1)
            link(v.tensor_reduce(most[:], bank[4][:, 2 * NE:3 * NE], AX, ALU.max))
            v.tensor_copy(most_i[:], most[:]).then_inc(s_most, 1)
            link(v.memset(pick[:, :, NE, :].bitcast(F32), 0.0))

            def turned_lo(e, fb):
                dve.wait_ge(s_hth, FB * e + fb + 1)
                v.tensor_tensor(ht_l[:, fb % 2], bank[4][:].rearrange("p (c n) -> p c n", c=4),
                                ht_h[:, fb % 2].bitcast(F32), ALU.subtract).then_inc(s_htl, 1)

            def gathered_lo(count, g):
                dve.wait_ge(s_gath, count + g + 1)
                v.tensor_copy(xe_l[:, 4 * (g - 2):4 * (g - 2) + 4, :],
                              bank[5][:].rearrange("p (c n) -> p c n", c=4)).then_inc(s_xe, 1)

            def experts(r):
                if r:
                    v.tensor_scalar(slot_of[:], slot_of[:], -float(P), None, ALU.add).then_inc(s_slot, 1)
                dve.wait_ge(s_slot, r + 1)
                for t in range(2):
                    for e in range(NE):
                        v.tensor_scalar(pick[:, t, e, :], const("iota"), slot_of[:, t, e:e + 1],
                                        chosen[:, t, e:e + 1], ALU.is_equal, ALU.mult).then_inc(s_pick, 1)
                for g in (2, 3):
                    gathered_lo(4 * (NE + 1) * r, g)
                with dve.Fori(0, NE) as el:
                    e = el + NE * r
                    for u, (kind, fb, part) in enumerate(ORDER):
                        n = U_MOE + EXPERT_UNITS * e + u
                        if (kind, part) == ("up", 1):
                            dve.wait_ge(s_used, 2 * n + 2)
                            dve.wait_ge(s_silu, 2 + FB * e + fb + 1)
                            v.tensor_tensor(hid_e[:, fb % 2, :], bank[2 + fb % 2][:], silu_g[:, fb % 2, :],
                                            ALU.mult).then_inc(s_mult, 1)
                        if (kind, fb, part) == ("down", FB - 1, 1):
                            dve.wait_ge(s_used, 2 * n + 2)
                            v.tensor_copy(y[:, bass.ds(el, 1), 512:D],
                                          bank[7][:].rearrange("p (a n) -> p a n", a=1)).then_inc(s_yfree, 1)
                        split_lo(n + 2, moe_slot((u + 2) % EXPERT_UNITS), u % 2)
                        if (kind, part) == ("gate", 1) and fb:
                            turned_lo(e, fb - 1)
                        if (kind, fb, part) == ("down", FB - 2, 1):
                            turned_lo(e, FB - 1)
                            gathered_lo(4 * (e + 1) + 4 * r, 2)
                        if (kind, fb, part) == ("down", FB - 1, 0):
                            gathered_lo(4 * (e + 1) + 4 * r, 3)
                for g in range(4):
                    dve.wait_ge(s_comb_done, 4 * r + g + 1)
                    part = acc[:, g // 2, 512 * (g % 2):512 * (g % 2 + 1)]
                    if r == 0:
                        dve.wait_ge(s_acc, 4)
                    v.tensor_tensor(part, part, bank[g][:], ALU.add).then_inc(s_accs, 1)
                dve.wait_ge(s_accs, 4 * (r + 1))

            experts(0)
            overflow(dve, lambda: experts(1))
            dve.sem_inc(s_done, 1)
            dve.wait_ge(s_fstd, 1)
            v.reciprocal(final_rstd[:], final_std[:]).then_inc(s_done, 1)
            dve.wait_ge(s_done, 2)
            for t in range(2):
                v.scalar_tensor_tensor(out=acc[:, t, :], in0=acc[:, t, :], scalar=final_rstd[:, t:t + 1],
                                       in1=param("final_norm"), op0=ALU.mult, op1=ALU.mult).then_inc(s_out, 1)

        @block.gpsimd
        def _(pool):
            def placed_gates(r):
                pool.wait_ge(s_slot, r + 1)
                pool.wait_ge(s_comb, 1)
                if r:
                    pool.wait_ge(s_comb_done, 4)
                for t in range(2):
                    for e in range(NE):
                        nc.gpsimd.tensor_scalar(placed[:, t, e, :], const("iota"), slot_of[:, t, e:e + 1],
                                                combine[:, t, e:e + 1], ALU.is_equal, ALU.mult).then_inc(s_placed, 1)

            placed_gates(0)
            overflow(pool, lambda: placed_gates(1))

        @block.tensor
        def _(pe):
            mm = nc.tensor.matmul

            def dense_unit(n, parity, banks, width, moving, chunks, first, last):
                for x in range(2):
                    at = 2 * parity + x
                    todo = [c for c in chunks if c // 4 == x]
                    for part, ready in ((hi, s_hi), (lo, s_lo)):
                        pe.wait_ge(ready, 2 * n + x + 1)
                        for j in range(2):
                            dst = bank[banks[j]][:, 0:width]
                            for c in todo:
                                w = part[:, at, 256 * (c % 4) + P * j:256 * (c % 4) + P * (j + 1)]
                                begin = first and part is hi and c == 0
                                end = last and part is lo and c == chunks[-1]
                                ins = mm(dst, w, moving(0, c), start=begin, stop=end)
                                if part is hi:
                                    ins = mm(dst, w, moving(1, c), start=False, stop=False)
                    ins.then_inc(s_used, 1)

            def stream(t0=0):
                return lambda part, c: (xh, xl)[part][:, c, t0:L]

            def square_sums(k, t0):
                pe.wait_ge(s_sq, k + 1)
                for c in range(DC):
                    ins = mm(bank[7][:, 0:L - t0], const("ones"), xn[:, c, t0:L], start=(c == 0), stop=(c == DC - 1))
                ins.then_inc(s_ss, 1)

            every = list(range(DC))
            pe.wait_ge(s_stream, 48)
            square_sums(0, 0)
            pe.wait_ge(s_xl, DC)
            with pe.Fori(0, 3) as i:
                for s in range(4):
                    pe.wait_ge(s_tile_dve, 8 * i + 2 * s + 2)
                    dense_unit(U_IN + 4 * i + s, s % 2, (2 * s, 2 * s + 1), L, stream(), every, True, True)
            pe.wait_ge(s_yl, DC)
            for m in range(N_OUT):
                pe.wait_ge(s_tile_dve, 24 + 2 * m + 2)
                dense_unit(U_OUT + m, m % 2, (2 * m, 2 * m + 1), L, lambda part, c: (yh, yl)[part][:, c, :],
                           every, True, True)
            square_sums(1, 0)
            pe.wait_ge(s_xl, 2 * DC)
            with pe.Fori(0, 7) as i:
                for s in range(4):
                    p = 2 * i + s // 2
                    pe.wait_ge((s_tile_act, s_hid)[s % 2], 2 * p + 2)
                    dense_unit(U_UP + 4 * i + s, s % 2, (2 * s, 2 * s + 1), L, stream(), every, True, True)
            pe.wait_ge(s_hid, 4 + 2 * 13)
            with pe.Fori(0, 2) as qq:
                for q in range(2):
                    pe.wait_ge(s_tile_dve, 38 + 4 * qq + 2 * q)
                    for m in range(4):
                        pe.wait_ge(s_hidl, 2 + 7 * m + 7)
                        dense_unit(U_DOWN + 8 * qq + 4 * q + m, m % 2, (2 * q, 2 * q + 1), L,
                                   lambda part, c, m=m: (hid_h, hid_l)[part][:, 7 * m + c, :],
                                   list(range(7)), m == 0, m == 3)
            square_sums(2, 0)
            pe.wait_ge(s_xl, 3 * DC)
            for m in range(N_QKV):
                if m >= 4:
                    pe.wait_ge(s_tile_act, 32 + 2 * (m - 4) + 2)
                t0 = 0 if m < 2 else META
                dense_unit(U_QKV + m, m % 2, (2 * m % 8, 2 * m % 8 + 1), L - t0, stream(t0), every, True, True)

            pe.wait_ge(s_tile_act, 44)
            for r in range(8):
                g = r // 2
                mm(bank[r][:, 0:L], const(("k_dup", "k_swap")[r % 2] + str(g % 2)), kv_t[:, g // 2, :],
                   start=True, stop=True).then_inc(s_rope, 1)
            for b in range(DC):
                pe.wait_ge(s_rope_read, b + 1)
                mm(bank[b][:, 0:SEQ], const("q_swap"), q_t[:, b, :], start=True, stop=True).then_inc(s_rope, 1)
            pe.wait_ge(s_rope_read, 9)
            for c in range(2):
                ins = nc.tensor.transpose(bank[0][0:META, P * c:P * (c + 1)], kv_t[:, 2 + c, 0:META], ident)
            ins.then_inc(s_v, 1)
            pe.wait_ge(s_rope_read, 10)
            for t in range(2):
                for c in range(2):
                    at = 2 * P * t + P * c
                    ins = nc.tensor.transpose(bank[1][:, at:at + P], kv_t[:, 2 + c, META + P * t:META + P * (t + 1)],
                                              ident)
            ins.then_inc(s_v, 1)

            def scores(s):
                t, b = s // 8, s % 8
                k0, k1 = ((0, META + P), (META, L))[t]
                if s >= 2:
                    pe.wait_ge(s_masked, s - 1)
                for i in range(2):
                    dst = bank[2 + s % 2][:, 2 * P * (i + 1) - (k1 - k0):2 * P * (i + 1)]
                    ins = mm(dst, q_rot[:, b, P * t:P * (t + 1)], k_rot[:, b // 2, i, k0:k1], start=True, stop=True)
                ins.then_inc(s_score, 1)

            def turn_probs(s):
                pe.wait_ge(s_exp, 2 * (s + 1))
                if s >= 2:
                    pe.wait_ge(s_pt_sb, 2 * (s - 1))
                dst = bank[4 + s % 2][:].rearrange("p (i k q) -> p i k q", i=2, k=2)
                for i in range(2):
                    for k in range(2):
                        n = META if s < 8 and k == 0 else P
                        ins = nc.tensor.transpose(dst[0:n, i, k, :], prob[:, s % 2, i, P * (k + 1) - n:P * (k + 1)],
                                                  ident)
                ins.then_inc(s_pt, 1)

            def sum_values(s):
                t, b = s // 8, s % 8
                pe.wait_ge(s_pt_sb, 2 * (s + 1))
                if s == 0:
                    pe.wait_ge(s_v_sb, 2)
                at = slice(HD * (b // 2), HD * (b // 2 + 1))
                values = ((v_meta[:, at], v_tok[:, 0, at]), (v_tok[:, 0, at], v_tok[:, 1, at]))[t]
                for i in range(2):
                    head = 2 * b + i
                    dst = bank[((6, 7), (0, 1))[t][head // 8]][:, HD * (head % 8):HD * (head % 8 + 1)]
                    for k in range(2):
                        n = META if t == 0 and k == 0 else P
                        ins = mm(dst, prob_t[0:n, s % 2, 2 * i + k, :], values[k], start=(k == 0), stop=(k == 1))
                ins.then_inc(s_pv, 1)

            pe.wait_ge(s_rot, 16)
            for s in range(18):
                if s < 16:
                    scores(s)
                if 1 <= s < 17:
                    turn_probs(s - 1)
                if s >= 2:
                    sum_values(s - 2)
            for g in range(4):
                t, q = g // 2, g % 2
                pe.wait_ge(s_o, g + 1)
                for c in range(4):
                    at = 512 * q + P * c
                    ins = nc.tensor.transpose(bank[(6, 7, 0, 1)[g]][:, P * c:P * (c + 1)], o_tok[:, t, at:at + P], ident)
                ins.then_inc(s_ot, 1)
            pe.wait_ge(s_ol, 4)
            for m in range(N_O):
                dense_unit(U_O + m, m % 2, (2 * m, 2 * m + 1), SEQ, lambda part, c: (oh, ol)[part][:, c, :],
                           every, True, True)

            pe.wait_ge(s_tile_dve, 56)
            for g in range(4):
                for c in range(4):
                    at = META + P * (g // 2)
                    ins = nc.tensor.transpose(bank[3 + g][:, P * c:P * (c + 1)], h[:, 4 * (g % 2) + c, at:at + P], ident)
                ins.then_inc(s_h_turned, 1)
            square_sums(3, META)
            pe.wait_ge(s_xn, 4 * DC)
            for g in range(4):
                for c in range(4):
                    at = META + P * (g // 2)
                    ins = nc.tensor.transpose(bank[(0, 1, 2, 7)[g]][:, P * c:P * (c + 1)],
                                              xn[:, 4 * (g % 2) + c, at:at + P], ident)
                ins.then_inc(s_xt, 1)
            pe.wait_ge(s_acc, 1)
            for t in range(2):
                for c in range(DC):
                    at = META + P * t
                    ins = mm(bank[3][:, NE * t:NE * (t + 1)], xn[:, c, at:at + P], param("router", NE * c, NE),
                             start=(c == 0), stop=(c == DC - 1))
            ins.then_inc(s_logit, 1)
            pe.wait_ge(s_chosen, 1)
            pe.wait_ge(s_acc, 2)
            mm(bank[4][:, 0:NE], const("before"), chosen[:, 0, :], start=True, stop=True)
            mm(bank[4][:, NE:2 * NE], const("ones"), chosen[:, 0, :], start=True, stop=False)
            mm(bank[4][:, NE:2 * NE], const("before"), chosen[:, 1, :], start=False, stop=True)
            mm(bank[4][:, 2 * NE:3 * NE], const("ones"), chosen_sum[:], start=True, stop=True).then_inc(s_pos, 1)

            def gather(count, g, e):
                src = (xt_h, xt_l)[g // 2]
                for c in range(4):
                    at = 512 * (g % 2) + P * c
                    for t in range(2):
                        slots = pick[:, t, e, :] if isinstance(e, int) else \
                            pick[:, t, bass.ds(e, 1), :].rearrange("p a n -> p (a n)")
                        ins = mm(bank[5][:, P * c:P * (c + 1)], src[:, t, at:at + P], slots,
                                 start=(t == 0), stop=(t == 1))
                ins.then_inc(s_gath, 1)

            def experts(r):
                pe.wait_ge(s_placed, 2 * NE * (r + 1))
                if r == 0:
                    pe.wait_ge(s_xtl, 4)
                    pe.wait_ge(s_acc, 4)
                else:
                    pe.wait_ge(s_accs, 4)
                for g in range(4):
                    for c in range(4):
                        ins = nc.tensor.transpose(bank[g][:, P * c:P * (c + 1)], placed[:, g // 2, 4 * (g % 2) + c, :],
                                                  ident)
                    ins.then_inc(s_place_t, 1)
                pe.wait_ge(s_pick, 2 * NE * (r + 1))
                before = 4 * (NE + 1) * r
                for g in range(4):
                    if before + g:
                        pe.wait_ge(s_xe, before + g)
                    gather(before, g, 0)
                pe.wait_ge(s_place, 4 * (r + 1))

                with pe.Fori(0, NE) as el:
                    e = el + NE * r
                    sets = 4 * (e + 1) + 4 * r

                    def turn_hidden(fb):
                        pe.wait_ge(s_mult, 2 + FB * e + fb + 1)
                        pe.wait_ge(s_htl, FB * e + fb + 1)
                        for c in range(4):
                            ins = nc.tensor.transpose(bank[4][:, P * c:P * (c + 1)],
                                                      hid_e[:, fb % 2, P * c:P * (c + 1)], ident)
                        ins.then_inc(s_ht, 1)

                    for u, (kind, fb, part) in enumerate(ORDER):
                        n = U_MOE + EXPERT_UNITS * e + u
                        if part == 0 and kind == "gate":
                            if fb == 0:
                                pe.wait_ge(s_xe, sets)
                            pe.wait_ge(s_silu, FB * e + fb + (1 if fb else 2))
                        if part == 0 and kind == "up":
                            pe.wait_ge(s_mult, FB * e + fb + (1 if fb else 2))
                        if part == 0 and kind == "down":
                            pe.wait_ge(s_htl, 1 + FB * e + fb + 1)
                            if fb == 0:
                                pe.wait_ge(s_yfree, 2 * e + 2)
                        for x in range(2):
                            at = 2 * (u % 2) + x
                            if kind == "down":
                                c = 2 * part + x
                                for w, ready in ((hi, s_hi), (lo, s_lo)):
                                    pe.wait_ge(ready, 2 * n + x + 1)
                                    for side in range(2):
                                        rhs = w[:, at, 512 * side:512 * (side + 1)]
                                        begin = fb == 0 and c == 0 and w is hi
                                        end = fb == FB - 1 and c == 3 and w is lo
                                        ins = mm(bank[6 + side][:], ht_h[:, fb % 2, c, :], rhs, start=begin, stop=end)
                                        if w is hi:
                                            mm(bank[6 + side][:], ht_l[:, fb % 2, c, :], rhs, start=False, stop=False)
                            else:
                                dst = bank[(0 if kind == "gate" else 2) + fb % 2][:]
                                for w, ready in ((hi, s_hi), (lo, s_lo)):
                                    pe.wait_ge(ready, 2 * n + x + 1)
                                    for k in range(2):
                                        c = 4 * part + 2 * x + k
                                        rhs = w[:, at, 512 * k:512 * (k + 1)]
                                        ins = mm(dst, xe_h[:, c, :], rhs, start=(c == 0 and w is hi),
                                                 stop=(c == DC - 1 and w is lo))
                                        if w is hi:
                                            mm(dst, xe_l[:, c, :], rhs, start=False, stop=False)
                            ins.then_inc(s_used, 1)
                        if (kind, part) == ("gate", 1) and fb:
                            turn_hidden(fb - 1)
                        if (kind, fb, part) == ("up", FB - 1, 1):
                            pe.wait_ge(s_xe, sets)
                            gather(sets, 0, el + 1)
                        if (kind, fb, part) == ("down", FB - 2, 0):
                            pe.wait_ge(s_xe, sets + 1)
                            gather(sets, 1, el + 1)
                        if (kind, fb, part) == ("down", FB - 2, 1):
                            turn_hidden(FB - 1)
                            pe.wait_ge(s_xe, sets + 2)
                            gather(sets, 2, el + 1)
                        if (kind, fb, part) == ("down", FB - 1, 0):
                            pe.wait_ge(s_xe, sets + 3)
                            gather(sets, 3, el + 1)

                pe.wait_ge(s_yfree, 2 + 2 * NE * (r + 1))
                for g in range(4):
                    t, side = g // 2, g % 2
                    for e in range(NE):
                        ins = mm(bank[g][:], place[:, e, P * t:P * (t + 1)], y[:, e, 512 * side:512 * (side + 1)],
                                 start=(e == 0), stop=(e == NE - 1))
                    ins.then_inc(s_comb_done, 1)

            experts(0)
            overflow(pe, lambda: experts(1))


def constants():
    import numpy as np

    c = np.zeros((P, N_CONSTS), np.float32)

    def part(name):
        at, n = CONSTS[name]
        return c[:, at:at + n]

    row = np.arange(P)
    part("ident")[:] = np.eye(P)
    partner = (row + HD // 2) % HD
    sign = np.where(row % HD < HD // 2, -1.0, 1.0)
    part("q_swap")[HD * (row // HD) + partner, row] = sign
    for i in range(2):
        part(f"k_dup{i}")[HD * i + row % HD, row] = 1.0
        part(f"k_swap{i}")[HD * i + partner, row] = sign
    part("before")[:] = row[:, None] < row[None, :]
    part("ones")[:] = 1.0
    part("iota")[:] = row[None, :]
    back = P + row[:, None] - np.arange(2 * P)[None, :]
    part("mask")[:] = np.where((back >= 0) & (back < WINDOW), 0.0, MASKED)
    freq = (np.float32(10000.0) ** (-np.arange(0, HD, 2, dtype=np.float32) / np.float32(HD))).astype(np.float32)
    angle = np.arange(L, dtype=np.float32)[None, :] * freq[row % (HD // 2)][:, None]
    part("cos")[:] = np.cos(angle)
    part("sin")[:] = np.sin(angle)
    own, other = np.divmod(np.arange(NE * NE), NE)
    part("earlier")[:] = (other < own)[None, :]
    part("eps")[:] = EPS
    return c


def kernel(x, meta_tokens, conv_norm, conv_w_in, conv_w, conv_w_out, ffn_norm, ffn_w_gate, ffn_w_up,
           ffn_w_down, attn_norm, attn_w_qkv, attn_b_qkv, attn_sinks, attn_w_o, moe_norm, moe_w_router,
           moe_w_gate, moe_w_up, moe_w_down, final_norm):
    import numpy as np
    import concourse.bacc as bacc
    from concourse.bass_utils import run_bass_kernel_spmd

    def columns(a):
        return np.asarray(a).reshape(-1, P).T

    x_t = np.ascontiguousarray(np.concatenate([np.asarray(meta_tokens), np.asarray(x)[0]], axis=0).T)
    params = np.concatenate([
        columns(conv_norm), columns(ffn_norm), columns(attn_norm), columns(moe_norm),
        columns(conv_w), columns(attn_b_qkv),
        np.broadcast_to(np.asarray(attn_sinks).reshape(1, NH), (P, NH)),
        np.asarray(moe_w_router).reshape(DC, P, NE).transpose(1, 0, 2).reshape(P, DC * NE),
        np.broadcast_to(np.asarray(final_norm).reshape(1, D), (P, D)),
    ], axis=1)
    arrays = {
        "x_t": x_t, "consts_d": constants(), "params_d": np.ascontiguousarray(params),
        "conv_w_in": np.asarray(conv_w_in)[0], "conv_w_out": np.asarray(conv_w_out)[0],
        "ffn_gate": np.asarray(ffn_w_gate)[0], "ffn_up": np.asarray(ffn_w_up)[0],
        "ffn_down": np.asarray(ffn_w_down)[0], "w_qkv": np.asarray(attn_w_qkv)[0], "w_o": np.asarray(attn_w_o)[0],
        "moe_gate": np.asarray(moe_w_gate).reshape(NE * D, FF), "moe_up": np.asarray(moe_w_up).reshape(NE * D, FF),
        "moe_down": np.asarray(moe_w_down).reshape(NE * FF, D),
    }
    arrays = {name: np.ascontiguousarray(a) for name, a in arrays.items()}
    nc = bacc.Bacc("TRN2", target_bir_lowering=False, num_devices=1)
    ins = {name: nc.dram_tensor(f"in_{name}", a.shape, mybir.dt.from_np(a.dtype), kind="ExternalInput").ap()
           for name, a in arrays.items()}
    out = nc.dram_tensor("out_dram", (1, SEQ, D), F32, kind="ExternalOutput").ap()
    trunk(nc, **ins, out=out)
    result = run_bass_kernel_spmd(nc, [{f"in_{name}": a for name, a in arrays.items()}], core_ids=[0])
    return result.results[0]["out_dram"]
```

```python
from contextlib import ExitStack

import concourse.bass as bass
from concourse import mybir

F32 = mybir.dt.float32
F32R = mybir.dt.float32r
I32 = mybir.dt.int32
ALU = mybir.AluOpType
ACT = mybir.ActivationFunctionType
AX = mybir.AxisListType.X

P = 128
D = 1024
SEQ = 256
META = 16
L = META + SEQ
DC = D // P
FF = 3584
FC = FF // P
FB = FF // 512
NE = 8
NH = 16
HD = 64
NKV = 4
WINDOW = 128
EPS = 1e-5
UNIT = 2048
HALF = UNIT // 2
SPLITS = 4
DENSE_RING = 4
RING = 7
MASKED = -1e30
STEPS = 16
PROBS = 4

N_IN, N_OUT, N_UP, N_DOWN, N_QKV, N_O = 12, 4, 28, 16, 6, 4
U_IN = 0
U_OUT = U_IN + N_IN
U_UP = U_OUT + N_OUT
U_DOWN = U_UP + N_UP
U_QKV = U_DOWN + N_DOWN
U_O = U_QKV + N_QKV
U_MOE = U_O + N_O
EXPERT_UNITS = 6 * FB
assert EXPERT_UNITS % RING == 0 and RING > DENSE_RING

CONSTS = {}
PARAMS = {}


def _columns(table, sizes):
    at = 0
    for name, n in sizes:
        table[name] = (at, n)
        at += n
    return at


N_CONSTS = _columns(CONSTS, [("ident", P), ("q_swap", P), ("k_dup0", P), ("k_dup1", P), ("k_swap0", P),
                             ("k_swap1", P), ("before", P), ("ones", P), ("iota", P), ("mask", 2 * P),
                             ("cos", L), ("sin", L), ("earlier", NE * NE), ("eps", 1)])
N_PARAMS = _columns(PARAMS, [("conv_norm", DC), ("ffn_norm", DC), ("attn_norm", DC), ("moe_norm", DC),
                             ("conv_w", 3 * DC), ("b_qkv", 12), ("sinks", NH), ("router", DC * NE),
                             ("final_norm", D)])


def expert_order():
    order = []
    for fb in range(FB):
        order += [("gate", fb, 0), ("gate", fb, 1), ("up", fb, 0), ("up", fb, 1)]
        if fb:
            order += [("down", fb - 1, 0), ("down", fb - 1, 1)]
    return order + [("down", FB - 1, 0), ("down", FB - 1, 1)]


ORDER = expert_order()
AT = {unit: n for n, unit in enumerate(ORDER)}


COMBINE_AT = [("up", 0, 1), ("gate", 1, 1), ("up", 1, 1), ("down", 0, 1)]
PLACE_AT = ("gate", 3, 1)
USES = 5
GATHERS = 5
GATHER_BANK = (1, 3, 5, 0, 2)


def gathered(r):
    return GATHERS * (NE + 1) * r


TURNS = [(side, what, t) for side in range(2) for what in range(3) for t in range(2)]
TURN_BANK = [g % 6 for g in range(12)]


def moe_slot(k):
    return (k + DENSE_RING) % RING


def dense_fills(slot):
    return len(range(slot, U_MOE, DENSE_RING)) if slot < DENSE_RING else 0


def dense_place(n):
    if n < U_MOE:
        return n % DENSE_RING, n // DENSE_RING + 1
    slot = moe_slot(n - U_MOE)
    return slot, dense_fills(slot) + (n - U_MOE) // RING + 1


def trunk(nc, x_t, consts_d, params_d, conv_w_in, conv_w_out, ffn_gate, ffn_up, ffn_down, w_qkv, w_o,
          moe_gate, moe_up, moe_down, out):
    ctx = ExitStack()
    with ctx:
        def sb(name, shape, dt=F32, scope=ctx):
            return scope.enter_context(nc.sbuf_tensor(name, shape, dt))

        def sem(name):
            return ctx.enter_context(nc.semaphore(name))

        consts = sb("consts", [P, N_CONSTS])
        params = sb("params", [P, N_PARAMS])
        h = sb("h", [P, DC, L])
        router_g = sb("router_g", [P, DC, NE])
        raw = sb("raw", [P, RING, UNIT])
        hi = sb("hi", [P, SPLITS, HALF], F32R)
        lo = sb("lo", [P, SPLITS, HALF], F32R)

        def const(name):
            at, n = CONSTS[name]
            return consts[:, at:at + n]

        def param(name, a=0, n=None):
            at, size = PARAMS[name]
            return params[:, at + a:at + (size if n is None else a + n)]

        ident = const("ident")

        with ExitStack() as dense:
            xn = sb("xn", [P, DC, L], scope=dense)
            xh = sb("xh", [P, DC, L], F32R, dense)
            xl = sb("xl", [P, DC, L], F32R, dense)
            rstd = sb("rstd", [P, L], scope=dense)
            with ExitStack() as s:
                u_act = sb("u_act", [P, DC, L], scope=s)
                v_act = sb("v_act", [P, DC, L + 2], scope=s)
                conv = sb("conv", [P, DC, L], scope=s)
                yh = sb("yh", [P, DC, L], F32R, s)
                yl = sb("yl", [P, DC, L], F32R, s)
            with ExitStack() as s:
                hid_h = sb("hid_h", [P, FC, L], F32R, s)
                hid_l = sb("hid_l", [P, FC, L], F32R, s)
                gate_act = sb("gate_act", [P, 2, L], scope=s)
                hid = sb("hid", [P, 2, L], scope=s)
            with ExitStack() as s:
                q_t = sb("q_t", [P, DC, SEQ], scope=s)
                q_rot = sb("q_rot", [P, DC, SEQ], scope=s)
                kv_t = sb("kv_t", [P, 4, L], scope=s)
                k_rot = sb("k_rot", [P, NKV, 2, L], scope=s)
                rope_a = sb("rope_a", [P, 2, L], scope=s)
                rope_b = sb("rope_b", [P, 2, L], scope=s)
                v_meta = sb("v_meta", [META, 4 * HD], scope=s)
                v_tok = sb("v_tok", [P, 2, 4 * HD], scope=s)
                prob = sb("prob", [P, PROBS, 2, SEQ], scope=s)
                prob_t = sb("prob_t", [P, 2, 4, P], scope=s)
                neg_max = sb("neg_max", [P, 2, NH], scope=s)
                neg_sink = sb("neg_sink", [P, NH], scope=s)
                row_max = sb("row_max", [P, 2], scope=s)
                prob_sum = sb("prob_sum", [P, 2, NH], scope=s)
                sink_exp = sb("sink_exp", [P, 2, NH], scope=s)
                oh = sb("oh", [P, DC, SEQ], F32R, s)
                ol = sb("ol", [P, DC, SEQ], F32R, s)

        o_tok = xn[:].rearrange("p c t -> p (c t)")[:, 0:2 * D].rearrange("p (t n) -> p t n", t=2)

        with ExitStack() as moe:
            silu_g = sb("silu_g", [P, 2, 512], scope=moe)
            hid_e = sb("hid_e", [P, 2, 512], scope=moe)
            ht_h = sb("ht_h", [P, 2, 4, P], F32R, moe)
            ht_l = sb("ht_l", [P, 2, 4, P], F32R, moe)
            xe_h = sb("xe_h", [P, DC, P], F32R, moe)
            xe_l = sb("xe_l", [P, DC, P], F32R, moe)
            y = sb("y", [P, D], scope=moe)
            xt_h = sb("xt_h", [P, 2, D], F32R, moe)
            xt_l = sb("xt_l", [P, 2, D], F32R, moe)
            acc = sb("acc", [P, 2, D], scope=moe)
            pick = sb("pick", [P, 2, P], F32R, moe)
            placed = sb("placed", [P, 2, P], scope=moe)
            place = sb("place", [P, SEQ], scope=moe)
            route = sb("route", [P, NE + 1, 4], scope=moe)
            gates = sb("gates", [P, NE, 2], scope=moe)
            tok_rstd = sb("tok_rstd", [P, 2], scope=moe)
            neg_top_r = sb("neg_top_r", [P, 2], scope=moe)
            slot_rstd = sb("slot_rstd", [P, 1], scope=moe)
            logit = sb("logit", [P, 2, NE], scope=moe)
            pair_a = sb("pair_a", [P, 2, NE, NE], scope=moe)
            pair_b = sb("pair_b", [P, 2, NE, NE], scope=moe)
            rank = sb("rank", [P, 2, NE], scope=moe)
            chosen = sb("chosen", [P, 2, NE], scope=moe)
            chosen_sum = sb("chosen_sum", [P, NE], scope=moe)
            combine = sb("combine", [P, 2, NE], scope=moe)
            top = sb("top", [P, 2], scope=moe)
            gate_sum = sb("gate_sum", [P, 2], scope=moe)
            most = sb("most", [P, 1], scope=moe)
            most_i = sb("most_i", [P, 1], I32, moe)
            sq_sum = sb("sq_sum", [P, 2], scope=moe)
            final_std = sb("final_std", [P, 2], scope=moe)
            final_rstd = sb("final_rstd", [P, 2], scope=moe)
            squares = sb("squares", [P, D], scope=moe)

        bank = [ctx.enter_context(nc.psum_tensor(f"bank{i}", [P, 512], F32)) for i in range(8)]

        s_stream = sem("stream_landed")
        s_raw = [sem(f"raw_landed{i}") for i in range(RING)]
        s_hi = sem("hi_ready")
        s_lo = sem("lo_ready")
        s_used = sem("half_used")
        s_sq = sem("squares_ready")
        s_ss = sem("square_sums_ready")
        s_std = sem("std_ready")
        s_xn = sem("xn_ready")
        s_xh = sem("xh_ready")
        s_xl = sem("xl_ready")
        s_tile_dve = sem("tiles_read_by_dve")
        s_tile_act = sem("tiles_read_by_act")
        s_yh = sem("yh_ready")
        s_yl = sem("yl_ready")
        s_hid = sem("hid_ready")
        s_hidh = sem("hid_h_ready")
        s_hidl = sem("hid_l_ready")
        s_rope = sem("rope_products")
        s_rope_read = sem("rope_read")
        s_rot = sem("rotated")
        s_v = sem("v_turned")
        s_v_sb = sem("v_ready")
        s_score = sem("scores_ready")
        s_masked = sem("scores_masked")
        s_negmax = sem("neg_max_ready")
        s_exp = sem("prob_ready")
        s_pt = sem("prob_turned")
        s_pt_sb = sem("prob_t_ready")
        s_pv = sem("values_summed")
        s_sink = sem("sink_shifted")
        s_sink_exp = sem("sink_exp_ready")
        s_o = sem("o_ready")
        s_ot = sem("o_turned")
        s_oh = sem("oh_ready")
        s_ol = sem("ol_ready")
        s_router = sem("router_g_ready")
        s_turned = sem("streams_turned")
        s_turn_read = sem("turned_read")
        s_tsq = sem("token_squares_ready")
        s_tstd = sem("token_std_ready")
        s_trstd = sem("token_rstd_ready")
        s_logit = sem("logits_ready")
        s_top = sem("top_ready")
        s_gexp = sem("gate_exp_ready")
        s_chosen = sem("chosen_ready")
        s_pos = sem("positions_ready")
        s_slot = sem("route_ready")
        s_comb = sem("combine_ready")
        s_pick = sem("pick_ready")
        s_placed = sem("placed_ready")
        s_zero = sem("zeroed")
        s_fill5 = sem("bank5_filled")
        s_read5 = sem("bank5_read")
        s_gath = sem("tokens_gathered")
        s_xe = sem("xe_ready")
        s_silu = sem("silu_ready")
        s_mult = sem("hidden_ready")
        s_ht = sem("hidden_turned")
        s_hth = sem("ht_h_ready")
        s_htl = sem("ht_l_ready")
        s_yfree = sem("y_banks_read")
        s_comb_done = sem("experts_summed")
        s_most = sem("most_ready")
        s_accs = sem("acc_summed")
        s_done = sem("moe_done")
        s_fsq = sem("final_squares_ready")
        s_fstd = sem("final_std_ready")
        s_out = sem("out_ready")
        s_stored = sem("out_stored")
        s_link = sem("dve_chain")

        w_in = conv_w_in.rearrange("(c p) n -> p c n", p=P)
        w_out = conv_w_out.rearrange("(c p) n -> p c n", p=P)
        w_fg = ffn_gate.rearrange("(c p) n -> p c n", p=P)
        w_fu = ffn_up.rearrange("(c p) n -> p c n", p=P)
        w_fd = ffn_down.rearrange("(m c p) n -> p m c n", p=P, c=7)
        w_qkv_v = w_qkv.rearrange("(c p) n -> p c n", p=P)
        w_o_v = w_o.rearrange("(c p) n -> p c n", p=P)
        out_v = out.rearrange("a (t p) d -> p (a t) d", p=P)

        def load_expert_unit(sp, e, u, wait):
            kind, fb, part = ORDER[u]
            slot = moe_slot(u)
            if wait is not None:
                if isinstance(wait, int) and wait < RING:
                    before = max(n for n in range(U_MOE) if n % DENSE_RING == slot)
                    sp.wait_ge(s_lo, 2 * before + 2)
                else:
                    sp.wait_ge(s_lo, 2 * (U_MOE + wait - RING) + 2)
            if kind == "down":
                src = moe_down[bass.ds(e * FF + 512 * fb + 256 * part, 256), :].rearrange("(c p) n -> p c n", p=P)
                dst = raw[:, slot, :].rearrange("p (c n) -> p c n", n=D)
            else:
                w = moe_gate if kind == "gate" else moe_up
                src = w[bass.ds(e * D + 512 * part, 512), 512 * fb:512 * (fb + 1)].rearrange(
                    "(c p) n -> p c n", p=P)
                dst = raw[:, slot, :].rearrange("p (c n) -> p c n", n=512)
            sp.dma_start(dst, src).then_inc(s_raw[slot], 16)

        def overflow(eng, body):
            eng.wait_ge(s_most, 1)
            count = eng.value_load(most_i[0:1, 0:1], min_val=0, max_val=SEQ)
            with eng.If(count > P):
                body()

        block = ctx.enter_context(nc.Block())

        @block.sync
        def _(sp):
            sp.dma_start(h[:], x_t.rearrange("(c p) t -> p c t", p=P)).then_inc(s_stream, 16)
            sp.dma_start(consts[:], consts_d).then_inc(s_stream, 16)
            sp.dma_start(params[:], params_d).then_inc(s_stream, 16)

            def load(n, slot, src, wait=True, size=UNIT):
                if wait:
                    sp.wait_ge(s_lo, 2 * n - 2 * DENSE_RING + 2)
                dst = raw[:, slot, 0:size].rearrange("p (c n) -> p c n", n=256)
                sp.dma_start(dst, src).then_inc(s_raw[slot], 16)

            for m in range(N_IN):
                at = D * (2 - m // 4) + 256 * (m % 4)
                load(U_IN + m, m % 4, w_in[:, :, at:at + 256], wait=m >= DENSE_RING)
            for k in range(RING - DENSE_RING):
                load_expert_unit(sp, 0, k, wait=None)
            for s in range(4):
                load(U_OUT + s, s, w_out[:, :, 256 * s:256 * (s + 1)])
            with sp.Fori(0, 7) as i:
                for s in range(4):
                    w = (w_fg, w_fu)[s % 2]
                    load(U_UP + 4 * i + s, s, w[:, :, bass.ds(512 * i + 256 * (s // 2), 256)])
            with sp.Fori(0, 4) as q:
                for s in range(4):
                    load(U_DOWN + 4 * q + s, s, w_fd[:, s, :, bass.ds(256 * q, 256)], size=7 * 256)
            for m in range(N_QKV):
                at = D + 256 * m if m < 2 else 256 * (m - 2)
                load(U_QKV + m, (U_QKV + m) % 4, w_qkv_v[:, :, at:at + 256])
            for m in range(N_O):
                load(U_O + m, (U_O + m) % 4, w_o_v[:, :, 256 * m:256 * (m + 1)])

            def experts(r):
                first = RING - DENSE_RING if r == 0 else 2
                for u in range(first, EXPERT_UNITS):
                    load_expert_unit(sp, 0, u, wait=r * NE * EXPERT_UNITS + u)
                with sp.Fori(1, NE) as e:
                    for u in range(EXPERT_UNITS):
                        load_expert_unit(sp, e, u, wait=(r * NE + e) * EXPERT_UNITS + u)
                for u in range(2):
                    load_expert_unit(sp, 0, u, wait=(r + 1) * NE * EXPERT_UNITS + u)

            experts(0)
            overflow(sp, lambda: experts(1))
            for t in range(2):
                sp.wait_ge(s_out, t + 1)
                sp.dma_start(out_v[:, t, :], acc[:, t, :]).then_inc(s_stored, 16)
            sp.wait_ge(s_stored, 32)

        @block.scalar
        def _(act):
            def split_hi(n, slot, parity, fill):
                act.wait_ge(s_raw[slot], 16 * fill)
                for x in range(2):
                    if not (isinstance(n, int) and 2 * n + x < SPLITS):
                        act.wait_ge(s_used, 2 * n + x - SPLITS + 1)
                    nc.scalar.copy(hi[:, 2 * parity + x, :],
                                   raw[:, slot, HALF * x:HALF * (x + 1)]).then_inc(s_hi, 1)

            def dense_hi(n):
                slot, fill = dense_place(n)
                split_hi(n, slot, n % 2, fill)

            def norm(k, t0, ready, ready_at, with_split):
                act.wait_ge(ready, ready_at)
                nc.scalar.activation(xn[:, :, t0:L], h[:, :, t0:L], ACT.Square).then_inc(s_sq, 1)
                if k == 0:
                    dense_hi(0)
                    dense_hi(1)
                act.wait_ge(s_ss, k + 1)
                nc.scalar.activation(rstd[:, t0:L], bank[7][:, 0:L - t0], ACT.Sqrt, bias=eps_col,
                                     scale=1.0 / D).then_inc(s_std, 1)
                if with_split:
                    for c in range(DC):
                        act.wait_ge(s_xn, DC * k + c + 1)
                        nc.scalar.copy(xh[:, c, :], xn[:, c, :]).then_inc(s_xh, 1)

            eps_col = const("eps")
            act.sem_inc(s_tile_act, 4)
            act.sem_inc(s_silu, 2)
            act.sem_inc(s_yfree, 2)
            norm(0, 0, s_stream, 48, True)

            for m in range(N_IN):
                n = U_IN + m
                if m >= 8:
                    for j in range(2):
                        blk = 2 * (m - 8) + j
                        act.wait_ge(s_tile_dve, 8 + 16 + blk + 1)
                        nc.scalar.copy(yh[:, blk, :], conv[:, blk, :]).then_inc(s_yh, 1)
                dense_hi(n + 2)
            for m in range(N_OUT):
                dense_hi(U_OUT + m + 2)
            norm(1, 0, s_tile_dve, 40, True)

            with act.Fori(0, 7) as i:
                for par in range(2):
                    p = 2 * i + par
                    gate_unit = U_UP + 4 * i + 2 * par
                    act.wait_ge(s_used, 2 * gate_unit + 2)
                    for j in range(2):
                        act.wait_ge(s_hid, 2 * p + j + 3)
                        nc.scalar.activation(gate_act[:, j, :], bank[4 * par + j][:, 0:L],
                                             ACT.Silu).then_inc(s_tile_act, 1)
                    for k in (2, 3):
                        ph = 2 * par + k
                        split_hi(gate_unit + k, ph % 4, ph % 2, U_UP // 4 + i + 1 + ph // 4)
                    for j in range(2):
                        act.wait_ge(s_hid, 4 + 2 * p + j + 1)
                        nc.scalar.copy(hid_h[:, bass.ds(2 * p + j, 1), :], hid[:, j:j + 1, :]).then_inc(s_hidh, 1)
            for m in range(N_DOWN):
                dense_hi(U_DOWN + m + 2)
            norm(2, 0, s_tile_dve, 48, True)

            for m in range(N_QKV):
                n = U_QKV + m
                act.wait_ge(s_used, 2 * n + 2)
                for j in range(2):
                    tile = 2 * m + j
                    src = bank[tile % 8]
                    if m < 2:
                        nc.scalar.activation(kv_t[:, tile, :], src[:, 0:L], ACT.Identity,
                                             bias=param("b_qkv", 8 + tile, 1)).then_inc(s_tile_act, 1)
                    else:
                        b = tile - 4
                        nc.scalar.activation(q_t[:, b, :], src[:, 0:SEQ], ACT.Identity,
                                             bias=param("b_qkv", b, 1)).then_inc(s_tile_act, 1)
                dense_hi(n + 2)
            act.wait_ge(s_v, 2)
            nc.scalar.copy(v_meta[:], bank[0][0:META, 0:256]).then_inc(s_v_sb, 1)
            nc.scalar.copy(v_tok[:].rearrange("p t n -> p (t n)"), bank[1][:, 0:512]).then_inc(s_v_sb, 1)

            def turned_probs(s):
                act.wait_ge(s_pt, s + 1)
                if s >= 2:
                    act.wait_ge(s_pv, s - 1)
                src = bank[4 + s % 2][:].rearrange("p (i k q) -> p i k q", i=2, k=2)
                dst = prob_t[:, s % 2].rearrange("p (i k) q -> p i k q", i=2)
                if s < 8:
                    nc.scalar.copy(dst[0:META, :, 0, :], src[0:META, :, 0, :]).then_inc(s_pt_sb, 1)
                    nc.scalar.copy(dst[:, :, 1, :], src[:, :, 1, :]).then_inc(s_pt_sb, 1)
                else:
                    nc.scalar.copy(dst, src).then_inc(s_pt_sb, 2)

            for s in range(STEPS):
                t, b = s // 8, s % 8
                k0 = P - META if t == 0 else 0
                if s >= 3:
                    turned_probs(s - 3)
                act.wait_ge(s_negmax, s + 1)
                for i in range(2):
                    nc.scalar.activation(prob[:, s % PROBS, i, k0:], prob[:, s % PROBS, i, k0:], ACT.Exp,
                                         bias=neg_max[:, t, 2 * b + i:2 * b + i + 1],
                                         accum_out=prob_sum[:, t, 2 * b + i:2 * b + i + 1]).then_inc(s_exp, 1)
            for s in range(STEPS - 3, STEPS):
                turned_probs(s)
            act.wait_ge(s_sink, 1)
            nc.scalar.activation(sink_exp[:].rearrange("p t n -> p (t n)"),
                                 sink_exp[:].rearrange("p t n -> p (t n)"), ACT.Exp).then_inc(s_sink_exp, 1)
            for g in range(4):
                t, q = g // 2, g % 2
                act.wait_ge(s_ot, g + 1)
                nc.scalar.copy(oh[:, 4 * q:4 * q + 4, P * t:P * (t + 1)],
                               bank[(6, 7, 0, 1)[g]][:].rearrange("p (c n) -> p c n", c=4)).then_inc(s_oh, 1)

            def turned_stream(g):
                side, what, t = TURNS[g]
                act.wait_ge(s_turned, g + 1)
                nc.scalar.copy((acc, xt_h, xt_l)[what][:, t, 512 * side:512 * (side + 1)],
                               bank[TURN_BANK[g]][:]).then_inc(s_turn_read, 1)

            for m in range(N_O):
                for j in range(2):
                    blk = 2 * m + j
                    act.wait_ge(s_tile_dve, 48 + blk + 1)
                    nc.scalar.activation(xh[:, blk, META:L], h[:, blk, META:L], ACT.Copy,
                                         scale=param("moe_norm", blk, 1)).then_inc(s_xh, 1)
                dense_hi(U_O + m + 2)
                if m == 2:
                    for g in range(4):
                        turned_stream(g)
            for g in range(4, 12):
                turned_stream(g)
            act.wait_ge(s_turn_read, 8)
            for t in range(2):
                if t:
                    act.wait_ge(s_tsq, 1)
                nc.scalar.activation(squares[:], acc[:, t, :], ACT.Square,
                                     accum_out=sq_sum[:, t:t + 1]).then_inc(s_tsq, 1)
            act.wait_ge(s_tsq, 2)
            nc.scalar.activation(final_std[:], sq_sum[:], ACT.Sqrt, bias=eps_col, scale=1.0 / D).then_inc(s_tstd, 1)
            act.wait_ge(s_top, 1)
            for t in range(2):
                nc.scalar.activation(combine[:, t, :], logit[:, t, :], ACT.Exp, bias=neg_top_r[:, t:t + 1],
                                     scale=tok_rstd[:, t:t + 1]).then_inc(s_gexp, 1)

            def turned_hi(e, fb):
                act.wait_ge(s_ht, FB * e + fb + 1)
                nc.scalar.copy(ht_h[:, fb % 2], bank[4][:].rearrange("p (c n) -> p c n", c=4)).then_inc(s_hth, 1)

            def gathered_hi(before, g):
                act.wait_ge(s_gath, before + g + 1)
                nc.scalar.copy(xe_h[:, 4 * g:4 * g + 4, :],
                               bank[GATHER_BANK[g]][:].rearrange("p (c n) -> p c n", c=4)).then_inc(s_xe, 1)

            def experts(r):
                for g in range(2):
                    gathered_hi(gathered(r), g)
                with act.Fori(0, NE) as el:
                    e = el + NE * r
                    use = USES * e
                    gath = GATHERS * (e + r + 1)
                    for u, (kind, fb, part) in enumerate(ORDER):
                        n = U_MOE + EXPERT_UNITS * e + u
                        if (kind, part) == ("gate", 1):
                            act.wait_ge(s_used, 2 * n + 2)
                            act.wait_ge(s_mult, FB * e + fb + (1 if fb else 2))
                            if fb == 0:
                                act.wait_ge(s_xe, gath)
                            nc.scalar.activation(silu_g[:, fb % 2, :], bank[fb % 2][:], ACT.Silu,
                                                 scale=slot_rstd[:]).then_inc(s_silu, 1)
                        if (kind, fb, part) == ("down", FB - 1, 1):
                            act.wait_ge(s_used, 2 * n + 2)
                            nc.scalar.copy(y[:, 0:512], bank[6][:]).then_inc(s_yfree, 1)
                        slot = moe_slot((u + 2) % EXPERT_UNITS)
                        fill = dense_fills(slot) + (EXPERT_UNITS // RING) * e + (u + 2) // RING + 1
                        split_hi(n + 2, slot, u % 2, fill)
                        if (kind, part) == ("gate", 1) and fb:
                            turned_hi(e, fb - 1)
                        if (kind, fb, part) == PLACE_AT:
                            act.wait_ge(s_fill5, use + 5)
                            nc.scalar.copy(place[:], bank[5][:, 0:SEQ]).then_inc(s_read5, 1)
                        if (kind, fb, part) == ("up", FB - 1, 1):
                            gathered_hi(gath, 0)
                            gathered_hi(gath, 1)
                        if (kind, fb, part) == ("down", FB - 2, 0):
                            turned_hi(e, FB - 1)

            experts(0)
            overflow(act, lambda: experts(1))
            act.wait_ge(s_done, 1)
            for t in range(2):
                if t:
                    act.wait_ge(s_fsq, 1)
                nc.scalar.activation(squares[:], acc[:, t, :], ACT.Square,
                                     accum_out=sq_sum[:, t:t + 1]).then_inc(s_fsq, 1)
            act.wait_ge(s_fsq, 2)
            nc.scalar.activation(final_std[:], sq_sum[:], ACT.Sqrt, bias=eps_col, scale=1.0 / D).then_inc(s_fstd, 1)

        @block.vector
        def _(dve):
            v = nc.vector
            links = [0]

            def link(ins):
                links[0] += 1
                ins.then_inc(s_link, 1)
                dve.wait_ge(s_link, links[0])

            def split_lo(n, slot, parity):
                for x in range(2):
                    dve.wait_ge(s_hi, 2 * n + x + 1)
                    at = 2 * parity + x
                    v.tensor_tensor(lo[:, at, :], raw[:, slot, HALF * x:HALF * (x + 1)], hi[:, at, :].bitcast(F32),
                                    ALU.subtract).then_inc(s_lo, 1)

            def dense_lo(n):
                split_lo(n, dense_place(n)[0], n % 2)

            def norm(k, t0, name, with_split):
                if k == 0:
                    dense_lo(0)
                    dense_lo(1)
                dve.wait_ge(s_std, k + 1)
                link(v.reciprocal(rstd[:, t0:L], rstd[:, t0:L]))

                def low(c):
                    dve.wait_ge(s_xh, DC * k + c + 1)
                    v.tensor_tensor(xl[:, c, :], xn[:, c, :], xh[:, c, :].bitcast(F32), ALU.subtract).then_inc(s_xl, 1)

                for c in range(DC):
                    v.scalar_tensor_tensor(out=xn[:, c, t0:L], in0=h[:, c, t0:L], scalar=param(name, c, 1),
                                           in1=rstd[:, t0:L], op0=ALU.mult, op1=ALU.mult).then_inc(s_xn, 1)
                    if with_split and c:
                        low(c - 1)
                if with_split:
                    low(DC - 1)

            dve.sem_inc(s_hid, 4)
            dve.sem_inc(s_hidl, 2)
            dve.sem_inc(s_mult, 2)
            dve.sem_inc(s_htl, 1)
            dve.sem_inc(s_read5, 1)
            v.memset(v_act[:, :, 0:2], 0.0).then_inc(s_tile_dve, 8)
            dve.wait_ge(s_stream, 48)
            v.tensor_tensor(router_g[:], param("router").rearrange("p (c n) -> p c n", n=NE),
                            param("moe_norm").unsqueeze(2).to_broadcast([P, DC, NE]), ALU.mult).then_inc(s_router, 1)
            norm(0, 0, "conv_norm", True)

            for m in range(N_IN):
                n = U_IN + m
                dve.wait_ge(s_used, 2 * n + 2)
                for j in range(2):
                    tile = 2 * m + j
                    blk = tile % 8
                    src = bank[blk][:, 0:L]
                    if m < 4:
                        v.tensor_copy(u_act[:, blk, :], src).then_inc(s_tile_dve, 1)
                    elif m < 8:
                        v.tensor_tensor(v_act[:, blk, 2:], src, u_act[:, blk, :], ALU.mult).then_inc(s_tile_dve, 1)
                    else:
                        v.tensor_tensor(conv[:, blk, :], src, conv[:, blk, :], ALU.mult).then_inc(s_tile_dve, 1)
                dense_lo(n + 2)
                for j in range(2):
                    tile = 2 * m + j
                    blk = tile % 8
                    if 4 <= m < 8:
                        dve.wait_ge(s_tile_dve, 8 + tile + 1)
                        link(v.tensor_scalar(conv[:, blk, :], v_act[:, blk, 0:L], param("conv_w", blk, 1), None,
                                             ALU.mult))
                        for k in (1, 2):
                            link(v.scalar_tensor_tensor(out=conv[:, blk, :], in0=v_act[:, blk, k:k + L],
                                                        scalar=param("conv_w", DC * k + blk, 1),
                                                        in1=conv[:, blk, :], op0=ALU.mult, op1=ALU.add))
                    elif m >= 8:
                        dve.wait_ge(s_yh, blk + 1)
                        v.tensor_tensor(yl[:, blk, :], conv[:, blk, :], yh[:, blk, :].bitcast(F32),
                                        ALU.subtract).then_inc(s_yl, 1)

            def add_tile(tile, src, t0):
                v.tensor_tensor(h[:, tile, t0:L], h[:, tile, t0:L], src[:, 0:L - t0], ALU.add).then_inc(s_tile_dve, 1)

            for m in range(N_OUT):
                dve.wait_ge(s_used, 2 * (U_OUT + m) + 2)
                for j in range(2):
                    add_tile(2 * m + j, bank[2 * m + j], 0)
                dense_lo(U_OUT + m + 2)
            norm(1, 0, "ffn_norm", True)

            with dve.Fori(0, 7) as i:
                for par in range(2):
                    p = 2 * i + par
                    gate_unit = U_UP + 4 * i + 2 * par
                    split_lo(gate_unit + 2, (2 * par + 2) % 4, 0)
                    dve.wait_ge(s_used, 2 * gate_unit + 4)
                    for j in range(2):
                        dve.wait_ge(s_tile_act, 4 + 2 * p + j + 1)
                        dve.wait_ge(s_hidl, 2 * p + j + 1)
                        v.tensor_tensor(hid[:, j, :], bank[4 * par + 2 + j][:, 0:L], gate_act[:, j, :],
                                        ALU.mult).then_inc(s_hid, 1)
                    split_lo(gate_unit + 3, (2 * par + 3) % 4, 1)
                    for j in range(2):
                        dve.wait_ge(s_hidh, 2 * p + j + 1)
                        f = bass.ds(2 * p + j, 1)
                        v.tensor_tensor(hid_l[:, f, :], hid[:, j:j + 1, :], hid_h[:, f, :].bitcast(F32),
                                        ALU.subtract).then_inc(s_hidl, 1)

            for m in range(N_DOWN):
                if m % 4 == 3:
                    q = m // 4
                    dve.wait_ge(s_used, 2 * (U_DOWN + m) + 2)
                    for j in range(2):
                        add_tile(2 * q + j, bank[2 * (q % 2) + j], 0)
                dense_lo(U_DOWN + m + 2)
            norm(2, 0, "attn_norm", True)

            for m in range(N_QKV):
                dense_lo(U_QKV + m + 2)
            link(v.memset(k_rot[:], 0.0))
            link(v.tensor_scalar(neg_sink[:], param("sinks"), -1.0, None, ALU.mult))
            cos, sin = const("cos"), const("sin")
            for g in range(NKV):
                if g >= 2:
                    dve.wait_ge(s_rot, 2 * g - 2)
                dve.wait_ge(s_rope, 2 * g + 1)
                v.tensor_tensor(rope_a[:, g % 2, :], bank[2 * g][:, 0:L], cos, ALU.mult).then_inc(s_rope_read, 1)
                dve.wait_ge(s_rope, 2 * g + 2)
                v.tensor_tensor(rope_b[:, g % 2, :], bank[2 * g + 1][:, 0:L], sin, ALU.mult).then_inc(s_rope_read, 1)
                dve.wait_ge(s_rope_read, 2 * g + 2)
                for i in range(2):
                    half = slice(HD * i, HD * (i + 1))
                    ins = v.tensor_tensor(k_rot[half, g, i, :], rope_a[half, g % 2, :], rope_b[half, g % 2, :],
                                          ALU.add)
                    ins.then_inc(s_rot, 1)
            dve.wait_ge(s_tile_act, 44)
            for b in range(DC):
                dve.wait_ge(s_rot, 6 + 2 * b if b < 2 else 8 + b - 1)
                link(v.tensor_tensor(rope_a[:, b % 2, 0:SEQ], q_t[:, b, :], cos[:, META:L], ALU.mult))
                dve.wait_ge(s_rope, 8 + b + 1)
                v.tensor_tensor(rope_b[:, b % 2, 0:SEQ], bank[b][:, 0:SEQ], sin[:, META:L],
                                ALU.mult).then_inc(s_rope_read, 1)
                dve.wait_ge(s_rope_read, 8 + b + 1)
                v.tensor_tensor(q_rot[:, b, :], rope_a[:, b % 2, 0:SEQ], rope_b[:, b % 2, 0:SEQ],
                                ALU.add).then_inc(s_rot, 1)

            def part_of(s):
                return prob[:, s % PROBS, :, P - META if s < 8 else 0:]

            def mask_scores(s):
                k0 = P - META if s < 8 else 0
                width = 2 * P - k0
                dve.wait_ge(s_score, s + 1)
                if s >= PROBS:
                    dve.wait_ge(s_pt, s - PROBS + 1)
                mask = const("mask")[:, k0:].unsqueeze(1).to_broadcast([P, 2, width])
                scores = bank[2 + s % 2][:].rearrange("p (i k) -> p i k", i=2)[:, :, k0:]
                v.scalar_tensor_tensor(out=part_of(s), in0=scores, scalar=HD ** -0.5, in1=mask, op0=ALU.mult,
                                       op1=ALU.add).then_inc(s_masked, 1)

            def find_max(s):
                t, b = s // 8, s % 8
                dve.wait_ge(s_masked, s + 1)
                if s:
                    dve.wait_ge(s_negmax, s)
                link(v.tensor_reduce(row_max[:], part_of(s), AX, ALU.max))
                v.scalar_tensor_tensor(out=neg_max[:, t, 2 * b:2 * b + 2], in0=row_max[:], scalar=-1.0,
                                       in1=neg_sink[:, 2 * b:2 * b + 2], op0=ALU.mult,
                                       op1=ALU.min).then_inc(s_negmax, 1)

            for s in range(STEPS + 1):
                if s < STEPS:
                    mask_scores(s)
                if s:
                    find_max(s - 1)
            dve.wait_ge(s_negmax, 16)
            v.tensor_tensor(sink_exp[:], neg_max[:], param("sinks").unsqueeze(1).to_broadcast([P, 2, NH]),
                            ALU.add).then_inc(s_sink, 1)
            dve.wait_ge(s_exp, 32)
            dve.wait_ge(s_sink_exp, 1)
            link(v.tensor_tensor(sink_exp[:], sink_exp[:], prob_sum[:], ALU.add))
            link(v.reciprocal(sink_exp[:], sink_exp[:]))
            for g in range(4):
                t, q = g // 2, g % 2
                dve.wait_ge(s_pv, 8 * (t + 1))
                v.tensor_tensor(o_tok[:, t, 512 * q:512 * (q + 1)].rearrange("p (n d) -> p n d", d=HD),
                                bank[(6, 7, 0, 1)[g]][:].rearrange("p (n d) -> p n d", d=HD),
                                sink_exp[:, t, 8 * q:8 * q + 8].unsqueeze(2).to_broadcast([P, 8, HD]),
                                ALU.mult).then_inc(s_o, 1)
            for g in range(4):
                t, q = g // 2, g % 2
                dve.wait_ge(s_oh, g + 1)
                dst = (slice(None), slice(4 * q, 4 * q + 4), slice(P * t, P * (t + 1)))
                v.tensor_tensor(ol[dst], bank[(6, 7, 0, 1)[g]][:].rearrange("p (c n) -> p c n", c=4),
                                oh[dst].bitcast(F32), ALU.subtract).then_inc(s_ol, 1)
            for m in range(N_O):
                dve.wait_ge(s_used, 2 * (U_O + m) + 2)
                for j in range(2):
                    add_tile(2 * m + j, bank[2 * m + j], META)
                for j in range(2):
                    c = 2 * m + j
                    dve.wait_ge(s_xh, 3 * DC + c + 1)
                    v.scalar_tensor_tensor(out=xl[:, c, META:L], in0=h[:, c, META:L], scalar=param("moe_norm", c, 1),
                                           in1=xh[:, c, META:L].bitcast(F32), op0=ALU.mult,
                                           op1=ALU.subtract).then_inc(s_xl, 1)
                dense_lo(U_O + m + 2)

            def gathered_lo(before, g):
                dve.wait_ge(s_gath, before + g + 1)
                v.tensor_copy(xe_l[:, 4 * (g - 2):4 * (g - 2) + 4, :],
                              bank[GATHER_BANK[g]][:].rearrange("p (c n) -> p c n", c=4)).then_inc(s_xe, 1)

            def slot_scale(before):
                dve.wait_ge(s_gath, before + 5)
                v.tensor_copy(slot_rstd[:], bank[GATHER_BANK[4]][:, 0:1]).then_inc(s_xe, 1)

            dve.wait_ge(s_logit, 1)
            link(v.tensor_copy(logit[:].rearrange("p t n -> p (t n)"), bank[6][:, 0:2 * NE]))
            other = logit[:].unsqueeze(2).to_broadcast([P, 2, NE, NE])
            own = logit[:].unsqueeze(3).to_broadcast([P, 2, NE, NE])
            earlier = const("earlier").rearrange("p (a b) -> p a b", a=NE).unsqueeze(1).to_broadcast([P, 2, NE, NE])
            link(v.tensor_tensor(pair_b[:], other, own, ALU.is_equal))
            link(v.tensor_tensor(pair_a[:], other, own, ALU.is_gt))
            link(v.tensor_tensor(pair_b[:], pair_b[:], earlier, ALU.mult))
            link(v.tensor_tensor(pair_a[:], pair_a[:], pair_b[:], ALU.add))
            link(v.tensor_reduce(rank[:], pair_a[:], AX, ALU.add))
            link(v.memset(route[:, NE, :], 0.0))
            by_tile = route[:, 0:NE, :].rearrange("p e (k t) -> p k t e", k=2)
            v.tensor_scalar(by_tile[:, 1], rank[:], 1.5, None, ALU.is_lt).then_inc(s_chosen, 1)
            link(v.tensor_scalar(chosen[:], rank[:], 1.5, None, ALU.is_lt))
            v.tensor_tensor(chosen_sum[:], chosen[:, 0], chosen[:, 1], ALU.add).then_inc(s_chosen, 1)
            dve.wait_ge(s_pos, 1)
            v.tensor_copy(by_tile[:, 0], bank[7][:, 0:2 * NE].rearrange("p (t e) -> p t e", t=2)).then_inc(s_slot, 1)
            dve.wait_ge(s_tstd, 1)
            link(v.reciprocal(tok_rstd[:], final_std[:]))
            link(v.tensor_reduce(top[:], logit[:], AX, ALU.max))
            v.scalar_tensor_tensor(out=neg_top_r[:], in0=top[:], scalar=-1.0, in1=tok_rstd[:], op0=ALU.mult,
                                   op1=ALU.mult).then_inc(s_top, 1)
            for g in (2, 3):
                gathered_lo(gathered(0), g)
            slot_scale(gathered(0))
            dve.wait_ge(s_gexp, 2)
            link(v.tensor_tensor(combine[:], combine[:], chosen[:], ALU.mult))
            link(v.tensor_reduce(gate_sum[:], combine[:], AX, ALU.add))
            link(v.reciprocal(gate_sum[:], gate_sum[:]))
            v.tensor_tensor(gates[:].rearrange("p e t -> p t e"), combine[:],
                            gate_sum[:].unsqueeze(2).to_broadcast([P, 2, NE]), ALU.mult).then_inc(s_comb, 1)
            link(v.tensor_reduce(most[:], bank[7][:, 2 * NE:3 * NE], AX, ALU.max))
            v.tensor_copy(most_i[:], most[:]).then_inc(s_most, 1)

            def turned_lo(e, fb):
                dve.wait_ge(s_hth, FB * e + fb + 1)
                v.tensor_tensor(ht_l[:, fb % 2], bank[4][:].rearrange("p (c n) -> p c n", c=4),
                                ht_h[:, fb % 2].bitcast(F32), ALU.subtract).then_inc(s_htl, 1)

            def experts(r):
                if r:
                    v.tensor_scalar(route[:, 0:NE, 0:2], route[:, 0:NE, 0:2], -float(P), None,
                                    ALU.add).then_inc(s_slot, 1)
                    for g in (2, 3):
                        gathered_lo(gathered(r), g)
                    slot_scale(gathered(r))
                with dve.Fori(0, NE) as el:
                    e = el + NE * r
                    use = USES * e
                    gath = GATHERS * (e + r + 1)
                    for u, (kind, fb, part) in enumerate(ORDER):
                        n = U_MOE + EXPERT_UNITS * e + u
                        if (kind, part) == ("up", 1):
                            dve.wait_ge(s_used, 2 * n + 2)
                            dve.wait_ge(s_silu, 2 + FB * e + fb + 1)
                            v.scalar_tensor_tensor(out=hid_e[:, fb % 2, :], in0=bank[2 + fb % 2][:],
                                                   scalar=slot_rstd[:], in1=silu_g[:, fb % 2, :], op0=ALU.mult,
                                                   op1=ALU.mult).then_inc(s_mult, 1)
                        if (kind, fb, part) == ("down", FB - 1, 1):
                            dve.wait_ge(s_used, 2 * n + 2)
                            v.tensor_copy(y[:, 512:D], bank[7][:]).then_inc(s_yfree, 1)
                        split_lo(n + 2, moe_slot((u + 2) % EXPERT_UNITS), u % 2)
                        if (kind, part) == ("gate", 1) and fb:
                            turned_lo(e, fb - 1)
                        if (kind, fb, part) in COMBINE_AT:
                            g = COMBINE_AT.index((kind, fb, part))
                            dve.wait_ge(s_fill5, use + g + 1)
                            acc_part = acc[:, g // 2, 512 * (g % 2):512 * (g % 2 + 1)]
                            v.tensor_tensor(acc_part, acc_part, bank[5][:], ALU.add).then_inc(s_read5, 1)
                        if (kind, fb, part) == ("up", FB - 1, 1):
                            gathered_lo(gath, 2)
                        if (kind, fb, part) == ("down", FB - 2, 0):
                            turned_lo(e, FB - 1)
                        if (kind, fb, part) == ("down", FB - 2, 1):
                            gathered_lo(gath, 3)
                            slot_scale(gath)
                for g in range(4):
                    dve.wait_ge(s_comb_done, 4 * r + g + 1)
                    acc_part = acc[:, g // 2, 512 * (g % 2):512 * (g % 2 + 1)]
                    v.tensor_tensor(acc_part, acc_part, bank[g][:], ALU.add).then_inc(s_accs, 1)
                dve.wait_ge(s_accs, 4 * (r + 1))

            experts(0)
            overflow(dve, lambda: experts(1))
            dve.sem_inc(s_done, 1)
            dve.wait_ge(s_fstd, 1)
            v.reciprocal(final_rstd[:], final_std[:]).then_inc(s_done, 1)
            dve.wait_ge(s_done, 2)
            for t in range(2):
                v.scalar_tensor_tensor(out=acc[:, t, :], in0=acc[:, t, :], scalar=final_rstd[:, t:t + 1],
                                       in1=param("final_norm"), op0=ALU.mult, op1=ALU.mult).then_inc(s_out, 1)

        @block.gpsimd
        def _(pool):
            g = nc.gpsimd

            def pick_tokens(e):
                for t in range(2):
                    g.tensor_scalar(pick[:, t, :], const("iota"), route[:, e, t:t + 1], route[:, e, 2 + t:3 + t],
                                    ALU.is_equal, ALU.mult).then_inc(s_pick, 1)

            def experts(r):
                pool.wait_ge(s_turned, 12)
                if r:
                    pool.wait_ge(s_comb_done, 4)
                g.memset(y[:], 0.0).then_inc(s_zero, 1)
                g.memset(place[:], 0.0).then_inc(s_zero, 1)
                pool.wait_ge(s_slot, r + 1)
                pool.wait_ge(s_chosen, 2)
                pick_tokens(0)
                pool.wait_ge(s_comb, 1)
                for e in range(NE):
                    pool.wait_ge(s_gath, gathered(r) + GATHERS * (e + 1))
                    for t in range(2):
                        g.tensor_scalar(placed[:, t, :], const("iota"), route[:, e, t:t + 1], gates[:, e, t:t + 1],
                                        ALU.is_equal, ALU.mult).then_inc(s_placed, 1)
                    pick_tokens(e + 1)

            experts(0)
            overflow(pool, lambda: experts(1))

        @block.tensor
        def _(pe):
            mm = nc.tensor.matmul

            def dense_unit(n, parity, banks, width, moving, chunks, first, last):
                for x in range(2):
                    at = 2 * parity + x
                    todo = [c for c in chunks if c // 4 == x]
                    for part, ready in ((hi, s_hi), (lo, s_lo)):
                        pe.wait_ge(ready, 2 * n + x + 1)
                        for j in range(2):
                            dst = bank[banks[j]][:, 0:width]
                            for c in todo:
                                w = part[:, at, 256 * (c % 4) + P * j:256 * (c % 4) + P * (j + 1)]
                                begin = first and part is hi and c == 0
                                end = last and part is lo and c == chunks[-1]
                                ins = mm(dst, w, moving(0, c), start=begin, stop=end)
                                if part is hi:
                                    ins = mm(dst, w, moving(1, c), start=False, stop=False)
                    ins.then_inc(s_used, 1)

            def stream(t0=0):
                return lambda part, c: (xh, xl)[part][:, c, t0:L]

            def square_sums(k, t0):
                pe.wait_ge(s_sq, k + 1)
                for c in range(DC):
                    ins = mm(bank[7][:, 0:L - t0], const("ones"), xn[:, c, t0:L], start=(c == 0), stop=(c == DC - 1))
                ins.then_inc(s_ss, 1)

            every = list(range(DC))
            pe.wait_ge(s_stream, 48)
            square_sums(0, 0)
            pe.wait_ge(s_xl, DC)
            with pe.Fori(0, 3) as i:
                for s in range(4):
                    pe.wait_ge(s_tile_dve, 8 * i + 2 * s + 2)
                    dense_unit(U_IN + 4 * i + s, s % 2, (2 * s, 2 * s + 1), L, stream(), every, True, True)
            pe.wait_ge(s_yl, DC)
            for m in range(N_OUT):
                pe.wait_ge(s_tile_dve, 24 + 2 * m + 2)
                dense_unit(U_OUT + m, m % 2, (2 * m, 2 * m + 1), L, lambda part, c: (yh, yl)[part][:, c, :],
                           every, True, True)
            square_sums(1, 0)
            pe.wait_ge(s_xl, 2 * DC)
            with pe.Fori(0, 7) as i:
                for s in range(4):
                    p = 2 * i + s // 2
                    pe.wait_ge((s_tile_act, s_hid)[s % 2], 2 * p + 2)
                    dense_unit(U_UP + 4 * i + s, s % 2, (2 * s, 2 * s + 1), L, stream(), every, True, True)
            pe.wait_ge(s_hid, 4 + 2 * 13)
            with pe.Fori(0, 2) as qq:
                for q in range(2):
                    pe.wait_ge(s_tile_dve, 38 + 4 * qq + 2 * q)
                    for m in range(4):
                        pe.wait_ge(s_hidl, 2 + 7 * m + 7)
                        dense_unit(U_DOWN + 8 * qq + 4 * q + m, m % 2, (2 * q, 2 * q + 1), L,
                                   lambda part, c, m=m: (hid_h, hid_l)[part][:, 7 * m + c, :],
                                   list(range(7)), m == 0, m == 3)
            square_sums(2, 0)
            pe.wait_ge(s_xl, 3 * DC)
            for m in range(N_QKV):
                if m >= 4:
                    pe.wait_ge(s_tile_act, 32 + 2 * (m - 4) + 2)
                t0 = 0 if m < 2 else META
                dense_unit(U_QKV + m, m % 2, (2 * m % 8, 2 * m % 8 + 1), L - t0, stream(t0), every, True, True)

            pe.wait_ge(s_tile_act, 44)
            for r in range(8):
                g = r // 2
                mm(bank[r][:, 0:L], const(("k_dup", "k_swap")[r % 2] + str(g % 2)), kv_t[:, g // 2, :],
                   start=True, stop=True).then_inc(s_rope, 1)
            for b in range(DC):
                pe.wait_ge(s_rope_read, b + 1)
                mm(bank[b][:, 0:SEQ], const("q_swap"), q_t[:, b, :], start=True, stop=True).then_inc(s_rope, 1)
            pe.wait_ge(s_rope_read, 9)
            for c in range(2):
                ins = nc.tensor.transpose(bank[0][0:META, P * c:P * (c + 1)], kv_t[:, 2 + c, 0:META], ident)
            ins.then_inc(s_v, 1)
            pe.wait_ge(s_rope_read, 10)
            for t in range(2):
                for c in range(2):
                    at = 2 * P * t + P * c
                    ins = nc.tensor.transpose(bank[1][:, at:at + P], kv_t[:, 2 + c, META + P * t:META + P * (t + 1)],
                                              ident)
            ins.then_inc(s_v, 1)

            def scores(s):
                t, b = s // 8, s % 8
                k0, k1 = ((0, META + P), (META, L))[t]
                if s >= 2:
                    pe.wait_ge(s_masked, s - 1)
                for i in range(2):
                    dst = bank[2 + s % 2][:, 2 * P * (i + 1) - (k1 - k0):2 * P * (i + 1)]
                    ins = mm(dst, q_rot[:, b, P * t:P * (t + 1)], k_rot[:, b // 2, i, k0:k1], start=True, stop=True)
                ins.then_inc(s_score, 1)

            def turn_probs(s):
                pe.wait_ge(s_exp, 2 * (s + 1))
                if s >= 2:
                    pe.wait_ge(s_pt_sb, 2 * (s - 1))
                dst = bank[4 + s % 2][:].rearrange("p (i k q) -> p i k q", i=2, k=2)
                for i in range(2):
                    for k in range(2):
                        n = META if s < 8 and k == 0 else P
                        ins = nc.tensor.transpose(dst[0:n, i, k, :], prob[:, s % PROBS, i, P * (k + 1) - n:P * (k + 1)],
                                                  ident)
                ins.then_inc(s_pt, 1)

            def sum_values(s):
                t, b = s // 8, s % 8
                pe.wait_ge(s_pt_sb, 2 * (s + 1))
                if s == 0:
                    pe.wait_ge(s_v_sb, 2)
                at = slice(HD * (b // 2), HD * (b // 2 + 1))
                values = ((v_meta[:, at], v_tok[:, 0, at]), (v_tok[:, 0, at], v_tok[:, 1, at]))[t]
                for i in range(2):
                    head = 2 * b + i
                    dst = bank[((6, 7), (0, 1))[t][head // 8]][:, HD * (head % 8):HD * (head % 8 + 1)]
                    for k in range(2):
                        n = META if t == 0 and k == 0 else P
                        ins = mm(dst, prob_t[0:n, s % 2, 2 * i + k, :], values[k], start=(k == 0), stop=(k == 1))
                ins.then_inc(s_pv, 1)

            pe.wait_ge(s_rot, 16)
            for s in range(STEPS + 4):
                if s < STEPS:
                    scores(s)
                if 3 <= s < STEPS + 3:
                    turn_probs(s - 3)
                if s >= 4:
                    sum_values(s - 4)
            for g in range(4):
                t, q = g // 2, g % 2
                pe.wait_ge(s_o, g + 1)
                for c in range(4):
                    at = 512 * q + P * c
                    ins = nc.tensor.transpose(bank[(6, 7, 0, 1)[g]][:, P * c:P * (c + 1)], o_tok[:, t, at:at + P], ident)
                ins.then_inc(s_ot, 1)
            pe.wait_ge(s_ol, 4)

            def turn_stream(g):
                side, what, t = TURNS[g]
                at = META + P * t
                for c in range(4):
                    src = (h[:], xh[:].bitcast(F32), xl[:].bitcast(F32))[what][:, 4 * side + c, at:at + P]
                    ins = nc.tensor.transpose(bank[TURN_BANK[g]][:, P * c:P * (c + 1)], src, ident)
                ins.then_inc(s_turned, 1)

            for m in range(N_O):
                dense_unit(U_O + m, m % 2, (2 * m, 2 * m + 1), SEQ, lambda part, c: (oh, ol)[part][:, c, :],
                           every, True, True)
                if m == 2:
                    pe.wait_ge(s_xl, 3 * DC + 4)
                    for g in range(4):
                        turn_stream(g)
            pe.wait_ge(s_tile_dve, 54)
            for g in range(4, 6):
                turn_stream(g)
            pe.wait_ge(s_tile_dve, 56)
            pe.wait_ge(s_router, 1)
            for t in range(2):
                for c in range(DC):
                    at = META + P * t
                    ins = mm(bank[6][:, NE * t:NE * (t + 1)], h[:, c, at:at + P], router_g[:, c, :],
                             start=(c == 0), stop=(c == DC - 1))
            ins.then_inc(s_logit, 1)
            pe.wait_ge(s_xl, 4 * DC)
            for g in range(6, 12):
                pe.wait_ge(s_turn_read, g - 5)
                turn_stream(g)
            pe.wait_ge(s_chosen, 2)
            mm(bank[7][:, 0:NE], const("before"), chosen[:, 0, :], start=True, stop=True)
            mm(bank[7][:, NE:2 * NE], const("ones"), chosen[:, 0, :], start=True, stop=False)
            mm(bank[7][:, NE:2 * NE], const("before"), chosen[:, 1, :], start=False, stop=True)
            mm(bank[7][:, 2 * NE:3 * NE], const("ones"), chosen_sum[:], start=True, stop=True).then_inc(s_pos, 1)

            def gather(g):
                src = (xt_h, xt_l)[g // 2]
                for c in range(4):
                    at = 512 * (g % 2) + P * c
                    for t in range(2):
                        ins = mm(bank[GATHER_BANK[g]][:, P * c:P * (c + 1)], src[:, t, at:at + P], pick[:, t, :],
                                 start=(t == 0), stop=(t == 1))
                ins.then_inc(s_gath, 1)

            def slot_scales():
                for t in range(2):
                    ins = mm(bank[GATHER_BANK[4]][:, 0:1], pick[:, t, :].bitcast(F32), tok_rstd[:, t:t + 1],
                             start=(t == 0), stop=(t == 1))
                ins.then_inc(s_gath, 1)

            def combine_experts(dst, g, done):
                t, side = g // 2, g % 2
                mm(dst, place[:, P * t:P * (t + 1)], y[:, 512 * side:512 * (side + 1)], start=True,
                   stop=True).then_inc(done, 1)

            def experts(r):
                if r == 0:
                    pe.wait_ge(s_turn_read, 12)
                else:
                    pe.wait_ge(s_accs, 4)
                pe.wait_ge(s_pick, 2 * (NE + 1) * r + 2)
                for g in range(4):
                    gather(g)
                pe.wait_ge(s_top, 1)
                slot_scales()
                if r == 0:
                    pe.wait_ge(s_most, 1)
                pe.wait_ge(s_zero, 2 * (r + 1))

                with pe.Fori(0, NE) as el:
                    e = el + NE * r
                    use = USES * e

                    def turn_hidden(fb):
                        pe.wait_ge(s_mult, 2 + FB * e + fb + 1)
                        pe.wait_ge(s_htl, FB * e + fb + 1)
                        for c in range(4):
                            ins = nc.tensor.transpose(bank[4][:, P * c:P * (c + 1)],
                                                      hid_e[:, fb % 2, P * c:P * (c + 1)], ident)
                        ins.then_inc(s_ht, 1)

                    for u, (kind, fb, part) in enumerate(ORDER):
                        n = U_MOE + EXPERT_UNITS * e + u
                        if part == 0 and kind == "gate":
                            if fb == 0:
                                pe.wait_ge(s_xe, GATHERS * (e + r + 1))
                            pe.wait_ge(s_silu, FB * e + fb + (1 if fb else 2))
                        if part == 0 and kind == "up":
                            pe.wait_ge(s_mult, FB * e + fb + (1 if fb else 2))
                        if part == 0 and kind == "down":
                            pe.wait_ge(s_htl, 1 + FB * e + fb + 1)
                            if fb == 0:
                                pe.wait_ge(s_yfree, 2 * e + 2)
                        for x in range(2):
                            at = 2 * (u % 2) + x
                            if kind == "down":
                                c = 2 * part + x
                                for w, ready in ((hi, s_hi), (lo, s_lo)):
                                    pe.wait_ge(ready, 2 * n + x + 1)
                                    for side in range(2):
                                        rhs = w[:, at, 512 * side:512 * (side + 1)]
                                        begin = fb == 0 and c == 0 and w is hi
                                        end = fb == FB - 1 and c == 3 and w is lo
                                        ins = mm(bank[6 + side][:], ht_h[:, fb % 2, c, :], rhs, start=begin, stop=end)
                                        if w is hi:
                                            mm(bank[6 + side][:], ht_l[:, fb % 2, c, :], rhs, start=False, stop=False)
                            else:
                                dst = bank[(0 if kind == "gate" else 2) + fb % 2][:]
                                for w, ready in ((hi, s_hi), (lo, s_lo)):
                                    pe.wait_ge(ready, 2 * n + x + 1)
                                    for k in range(2):
                                        c = 4 * part + 2 * x + k
                                        rhs = w[:, at, 512 * k:512 * (k + 1)]
                                        ins = mm(dst, xe_h[:, c, :], rhs, start=(c == 0 and w is hi),
                                                 stop=(c == DC - 1 and w is lo))
                                        if w is hi:
                                            mm(dst, xe_l[:, c, :], rhs, start=False, stop=False)
                            ins.then_inc(s_used, 1)
                        if (kind, part) == ("gate", 1) and fb:
                            turn_hidden(fb - 1)
                        if (kind, fb, part) in COMBINE_AT:
                            g = COMBINE_AT.index((kind, fb, part))
                            pe.wait_ge(s_yfree, 2 * e + 2)
                            pe.wait_ge(s_read5, use + g + 1)
                            combine_experts(bank[5][:], g, s_fill5)
                        if (kind, fb, part) == PLACE_AT:
                            pe.wait_ge(s_placed, 2 * e + 2)
                            pe.wait_ge(s_read5, use + 5)
                            for t in range(2):
                                ins = nc.tensor.transpose(bank[5][:, P * t:P * (t + 1)], placed[:, t, :], ident)
                            ins.then_inc(s_fill5, 1)
                        if (kind, fb, part) == ("up", FB - 1, 1):
                            pe.wait_ge(s_pick, 2 * e + 2 * r + 4)
                            pe.wait_ge(s_read5, use + 6)
                            for g in range(3):
                                gather(g)
                        if (kind, fb, part) == ("down", FB - 2, 0):
                            turn_hidden(FB - 1)
                            gather(3)
                            slot_scales()

                pe.wait_ge(s_yfree, 2 + 2 * NE * (r + 1))
                for g in range(4):
                    combine_experts(bank[g][:], g, s_comb_done)

            experts(0)
            overflow(pe, lambda: experts(1))


def constants():
    import numpy as np

    c = np.zeros((P, N_CONSTS), np.float32)

    def part(name):
        at, n = CONSTS[name]
        return c[:, at:at + n]

    row = np.arange(P)
    part("ident")[:] = np.eye(P)
    partner = (row + HD // 2) % HD
    sign = np.where(row % HD < HD // 2, -1.0, 1.0)
    part("q_swap")[HD * (row // HD) + partner, row] = sign
    for i in range(2):
        part(f"k_dup{i}")[HD * i + row % HD, row] = 1.0
        part(f"k_swap{i}")[HD * i + partner, row] = sign
    part("before")[:] = row[:, None] < row[None, :]
    part("ones")[:] = 1.0
    part("iota")[:] = row[None, :]
    back = P + row[:, None] - np.arange(2 * P)[None, :]
    part("mask")[:] = np.where((back >= 0) & (back < WINDOW), 0.0, MASKED)
    freq = (np.float32(10000.0) ** (-np.arange(0, HD, 2, dtype=np.float32) / np.float32(HD))).astype(np.float32)
    angle = np.arange(L, dtype=np.float32)[None, :] * freq[row % (HD // 2)][:, None]
    part("cos")[:] = np.cos(angle)
    part("sin")[:] = np.sin(angle)
    own, other = np.divmod(np.arange(NE * NE), NE)
    part("earlier")[:] = (other < own)[None, :]
    part("eps")[:] = EPS
    return c


def kernel(x, meta_tokens, conv_norm, conv_w_in, conv_w, conv_w_out, ffn_norm, ffn_w_gate, ffn_w_up,
           ffn_w_down, attn_norm, attn_w_qkv, attn_b_qkv, attn_sinks, attn_w_o, moe_norm, moe_w_router,
           moe_w_gate, moe_w_up, moe_w_down, final_norm):
    import numpy as np
    import concourse.bacc as bacc
    from concourse.bass_utils import run_bass_kernel_spmd

    def columns(a):
        return np.asarray(a).reshape(-1, P).T

    x_t = np.ascontiguousarray(np.concatenate([np.asarray(meta_tokens), np.asarray(x)[0]], axis=0).T)
    params = np.concatenate([
        columns(conv_norm), columns(ffn_norm), columns(attn_norm), columns(moe_norm),
        columns(conv_w), columns(attn_b_qkv),
        np.broadcast_to(np.asarray(attn_sinks).reshape(1, NH), (P, NH)),
        np.asarray(moe_w_router).reshape(DC, P, NE).transpose(1, 0, 2).reshape(P, DC * NE),
        np.broadcast_to(np.asarray(final_norm).reshape(1, D), (P, D)),
    ], axis=1)
    arrays = {
        "x_t": x_t, "consts_d": constants(), "params_d": np.ascontiguousarray(params),
        "conv_w_in": np.asarray(conv_w_in)[0], "conv_w_out": np.asarray(conv_w_out)[0],
        "ffn_gate": np.asarray(ffn_w_gate)[0], "ffn_up": np.asarray(ffn_w_up)[0],
        "ffn_down": np.asarray(ffn_w_down)[0], "w_qkv": np.asarray(attn_w_qkv)[0], "w_o": np.asarray(attn_w_o)[0],
        "moe_gate": np.asarray(moe_w_gate).reshape(NE * D, FF), "moe_up": np.asarray(moe_w_up).reshape(NE * D, FF),
        "moe_down": np.asarray(moe_w_down).reshape(NE * FF, D),
    }
    arrays = {name: np.ascontiguousarray(a) for name, a in arrays.items()}
    nc = bacc.Bacc("TRN2", target_bir_lowering=False, num_devices=1)
    ins = {name: nc.dram_tensor(f"in_{name}", a.shape, mybir.dt.from_np(a.dtype), kind="ExternalInput").ap()
           for name, a in arrays.items()}
    out = nc.dram_tensor("out_dram", (1, SEQ, D), F32, kind="ExternalOutput").ap()
    trunk(nc, **ins, out=out)
    result = run_bass_kernel_spmd(nc, [{f"in_{name}": a for name, a in arrays.items()}], core_ids=[0])
    return result.results[0]["out_dram"]
```

```python
from contextlib import ExitStack

import concourse.bass as bass
from concourse import mybir

F32 = mybir.dt.float32
F32R = mybir.dt.float32r
I32 = mybir.dt.int32
ALU = mybir.AluOpType
ACT = mybir.ActivationFunctionType
AX = mybir.AxisListType.X

P = 128
D = 1024
SEQ = 256
META = 16
L = META + SEQ
DC = D // P
FF = 3584
FC = FF // P
FB = FF // 512
NE = 8
NH = 16
HD = 64
NKV = 4
WINDOW = 128
EPS = 1e-5
UNIT = 2048
HALF = UNIT // 2
SPLITS = 4
DENSE_RING = 4
RING = 7
PARKED = 3
MASKED = -1e30
ROPE_BANK = (6, 7, 4, 5, 6, 7, 0, 1)
STEPS = 16
PROBS = 4

N_IN, N_OUT, N_UP, N_DOWN, N_QKV, N_O = 12, 4, 28, 16, 6, 4
U_IN = 0
U_OUT = U_IN + N_IN
U_UP = U_OUT + N_OUT
U_DOWN = U_UP + N_UP
U_QKV = U_DOWN + N_DOWN
U_O = U_QKV + N_QKV
U_MOE = U_O + N_O
EXPERT_UNITS = 6 * FB
assert EXPERT_UNITS % RING == 0 and RING > DENSE_RING

CONSTS = {}
PARAMS = {}


def _columns(table, sizes):
    at = 0
    for name, n in sizes:
        table[name] = (at, n)
        at += n
    return at


N_CONSTS = _columns(CONSTS, [("ones", P), ("eps", 1), ("ident", P), ("q_swap", P), ("k_dup0", P), ("k_dup1", P), ("k_swap0", P),
                             ("k_swap1", P), ("before", P), ("iota", P), ("mask", 2 * P), ("cos", L), ("sin", L),
                             ("earlier", NE * NE)])
FIRST_CONSTS = P + 1
N_PARAMS = _columns(PARAMS, [("conv_norm", DC), ("ffn_norm", DC), ("attn_norm", DC), ("moe_norm", DC),
                             ("conv_w", 3 * DC), ("b_qkv", 12), ("sinks", NH), ("router", DC * NE),
                             ("final_norm", D)])
FIRST_PARAMS = 7 * DC


def expert_order():
    order = []
    for fb in range(FB):
        order += [("gate", fb, 0), ("gate", fb, 1), ("up", fb, 0), ("up", fb, 1)]
        if fb:
            order += [("down", fb - 1, 0), ("down", fb - 1, 1)]
    return order + [("down", FB - 1, 0), ("down", FB - 1, 1)]


ORDER = expert_order()
AT = {unit: n for n, unit in enumerate(ORDER)}


COMBINE_AT = [("up", 0, 1), ("gate", 1, 1), ("up", 1, 1), ("down", 0, 1)]
PLACE_AT = ("gate", 3, 1)
USES = 5
GATHERS = 3
GATHER_BANK = (1, 3, 5)
SLOTS_BANK = (0, 2)


def gathered(r):
    return GATHERS * (NE + 1) * r


TURNS = [(0, 0, 0), (0, 0, 1), (0, 1, 0), (0, 1, 1), (1, 1, 0), (1, 1, 1), (1, 0, 0), (1, 0, 1)]
TURN_BANK = (0, 1, 2, 3, 4, 5, 0, 1)


def moe_slot(k):
    return (list(range(DENSE_RING, RING)) + [(U_O + m) % DENSE_RING for m in range(DENSE_RING)])[k % RING]


def dense_fills(slot):
    return len(range(slot, U_MOE, DENSE_RING)) if slot < DENSE_RING else 0


def dense_place(n):
    if n < U_MOE:
        return n % DENSE_RING, n // DENSE_RING + 1
    slot = moe_slot(n - U_MOE)
    return slot, dense_fills(slot) + (n - U_MOE) // RING + 1


def trunk(nc, x_t, consts_d, params_d, conv_w_in, conv_w_out, ffn_gate, ffn_up, ffn_down, w_qkv, w_o,
          moe_gate, moe_up, moe_down, out):
    ctx = ExitStack()
    with ctx:
        def sb(name, shape, dt=F32, scope=ctx):
            return scope.enter_context(nc.sbuf_tensor(name, shape, dt))

        def sem(name):
            return ctx.enter_context(nc.semaphore(name))

        consts = sb("consts", [P, N_CONSTS])
        params = sb("params", [P, N_PARAMS])
        h = sb("h", [P, DC, L])
        router_g = sb("router_g", [P, DC, NE])
        raw = sb("raw", [P, RING, UNIT])
        hi = sb("hi", [P, SPLITS, HALF], F32R)
        lo = sb("lo", [P, SPLITS, HALF], F32R)

        def const(name):
            at, n = CONSTS[name]
            return consts[:, at:at + n]

        def param(name, a=0, n=None):
            at, size = PARAMS[name]
            return params[:, at + a:at + (size if n is None else a + n)]

        ident = const("ident")

        with ExitStack() as dense:
            sq = sb("sq", [P, DC, L], scope=dense)
            rstd = sb("rstd", [P, L], scope=dense)
            with ExitStack() as stream:
                xh = sb("xh", [P, DC, L], F32R, stream)
                xl = sb("xl", [P, DC, L], F32R, stream)
                with ExitStack() as s:
                    rstd_sq = sb("rstd_sq", [P, L], scope=s)
                    u_act = sb("u_act", [P, DC, L], scope=s)
                    v_act = sb("v_act", [P, DC, L + 2], scope=s)
                    conv = sb("conv", [P, DC, L], scope=s)
                    yh = sb("yh", [P, DC, L], F32R, s)
                    yl = sb("yl", [P, DC, L], F32R, s)
                with ExitStack() as s:
                    hid_h = sb("hid_h", [P, FC, L], F32R, s)
                    hid_l = sb("hid_l", [P, FC, L], F32R, s)
                    gate_act = sb("gate_act", [P, 2, L], scope=s)
                    hid = sb("hid", [P, 2, L], scope=s)
                with ExitStack() as s:
                    q_t = sb("q_t", [P, DC, SEQ], scope=s)
                    q_rot = sb("q_rot", [P, DC, SEQ], scope=s)
                    kv_t = sb("kv_t", [P, 4, L], scope=s)
                    k_rot = sb("k_rot", [P, NKV, 2, L], scope=s)
                    q_sin = sb("q_sin", [P, 2, SEQ], scope=s)
                    neg_max = sb("neg_max", [P, 2, NH], scope=s)
                    row_max = sb("row_max", [P, 2], scope=s)
                    prob_sum = sb("prob_sum", [P, 2, NH], scope=s)
                    prob_scale = sb("prob_scale", [P, 2, NH], scope=s)
                    oh = sb("oh", [P, DC, SEQ], F32R, s)
                    ol = sb("ol", [P, DC, SEQ], F32R, s)
                    parked = sb("parked", [P, PARKED, UNIT], scope=s)
            with ExitStack() as s:
                prob = sb("prob", [P, PROBS, 2, SEQ + 1], scope=s)
                prob_t = sb("prob_t", [P, 2, 2, 2, P], scope=s)
                inverse = sb("inverse", [P, 2, 2, P], scope=s)
                v_meta = sb("v_meta", [META, NKV, 2, HD], scope=s)
            with ExitStack() as s:
                xg = sb("xg", [P, DC, SEQ], scope=s)

        sq_flat = sq[:].rearrange("p c t -> p (c t)")
        k_cos = sq_flat[:, 0:2 * L].rearrange("p (c t) -> p c t", c=2)
        k_sin = sq_flat[:, 2 * L:4 * L].rearrange("p (c t) -> p c t", c=2)
        v_tok = sq_flat[:, 4 * L:4 * L + 4 * SEQ].rearrange("p (t g i d) -> p t g i d", t=2, g=NKV, i=2)

        with ExitStack() as moe:
            silu_g = sb("silu_g", [P, 2, 512], scope=moe)
            hid_e = sb("hid_e", [P, 2, 512], scope=moe)
            ht_h = sb("ht_h", [P, 2, 4, P], F32R, moe)
            ht_l = sb("ht_l", [P, 2, 4, P], F32R, moe)
            xe_h = sb("xe_h", [P, DC, P], F32R, moe)
            xe_l = sb("xe_l", [P, DC, P], F32R, moe)
            y = sb("y", [P, D], scope=moe)
            xt_h = sb("xt_h", [P, 2, D], F32R, moe)
            xt_l = sb("xt_l", [P, 2, D], F32R, moe)
            xs = sb("xs", [P, D], scope=moe)
            acc = sb("acc", [P, 2, D], scope=moe)
            pick = sb("pick", [P, 2, P], F32R, moe)
            placed = sb("placed", [P, 2, P], scope=moe)
            place = sb("place", [P, SEQ], scope=moe)
            route = sb("route", [P, NE + 1, 4], scope=moe)
            gates = sb("gates", [P, NE, 2], scope=moe)
            tok_rstd = sb("tok_rstd", [P, 2], scope=moe)
            neg_top_r = sb("neg_top_r", [P, 2], scope=moe)
            slot_rstd = sb("slot_rstd", [P, 1], scope=moe)
            logit = sb("logit", [P, 2, NE], scope=moe)
            pair_a = sb("pair_a", [P, 2, NE, NE], scope=moe)
            pair_b = sb("pair_b", [P, 2, NE, NE], scope=moe)
            rank = sb("rank", [P, 2, NE], scope=moe)
            chosen = sb("chosen", [P, 2, NE], scope=moe)
            chosen_sum = sb("chosen_sum", [P, NE], scope=moe)
            combine = sb("combine", [P, 2, NE], scope=moe)
            top = sb("top", [P, 2], scope=moe)
            gate_sum = sb("gate_sum", [P, 2], scope=moe)
            most = sb("most", [P, 1], scope=moe)
            most_i = sb("most_i", [P, 1], I32, moe)
            sq_sum = sb("sq_sum", [P, 2], scope=moe)
            final_std = sb("final_std", [P, 2], scope=moe)
            final_rstd = sb("final_rstd", [P, 2], scope=moe)
            squares = sb("squares", [P, D], scope=moe)

        bank = [ctx.enter_context(nc.psum_tensor(f"bank{i}", [P, 512], F32)) for i in range(8)]

        s_h = [sem(f"x_landed{i}") for i in range(2)]
        s_first = sem("norm_weights_landed")
        s_ones = sem("ones_and_eps_landed")
        s_rest = sem("rest_landed")
        s_raw = [sem(f"raw_landed{i}") for i in range(RING)]
        s_parked = [sem(f"parked_landed{k}") for k in range(PARKED)]
        s_hi = sem("hi_ready")
        s_lo = sem("lo_ready")
        s_used = sem("half_used")
        s_sq = sem("squares_ready")
        s_sq_sum = sem("squares_summed_over_chunks")
        s_ss = sem("square_sums_ready")
        s_std = sem("std_ready")
        s_scaled = sem("tiles_times_rstd")
        s_xh = sem("xh_ready")
        s_xl = sem("xl_ready")
        s_tile_dve = sem("tiles_read_by_dve")
        s_tile_act = sem("tiles_read_by_act")
        s_yh = sem("yh_ready")
        s_yl = sem("yl_ready")
        s_hid = sem("hid_ready")
        s_hidh = sem("hid_h_ready")
        s_hidl = sem("hid_l_ready")
        s_kzero = sem("k_rot_zeroed")
        s_kcs = sem("k_cos_and_sin_ready")
        s_krope = sem("k_rotated")
        s_krot = sem("k_rot_ready")
        s_qcos = sem("q_cos_ready")
        s_rope = sem("q_turned")
        s_rope_read = sem("q_turned_read")
        s_rot = sem("q_rot_ready")
        s_v = sem("v_turned")
        s_v_sb = sem("v_ready")
        s_score = sem("scores_ready")
        s_masked = sem("scores_masked")
        s_negmax = sem("neg_max_ready")
        s_exp = sem("prob_ready")
        s_pt = sem("prob_turned")
        s_pt_sb = sem("prob_t_ready")
        s_pv = sem("values_summed")
        s_inverse = sem("inverse_ready")
        s_oh = sem("oh_ready")
        s_ol = sem("ol_ready")
        s_router = sem("router_g_ready")
        s_turned = sem("streams_turned")
        s_xg = sem("xg_ready")
        s_turn_read = sem("turned_read")
        s_xtl = sem("xt_l_ready")
        s_xs = sem("xs_ready")
        s_xst = sem("xs_turned")
        s_tsq = sem("token_squares_ready")
        s_tstd = sem("token_std_ready")
        s_logit = sem("logits_ready")
        s_top = sem("tok_rstd_and_top_ready")
        s_gexp = sem("gate_exp_ready")
        s_chosen = sem("chosen_ready")
        s_pos = sem("positions_ready")
        s_slot = sem("route_ready")
        s_comb = sem("combine_ready")
        s_pick = sem("pick_ready")
        s_placed = sem("placed_ready")
        s_zero = sem("zeroed")
        s_fill5 = sem("bank5_filled")
        s_read5 = sem("bank5_read")
        s_gath = sem("tokens_gathered")
        s_xeh = sem("xe_h_ready")
        s_xe = sem("xe_ready")
        s_silu = sem("silu_ready")
        s_mult = sem("hidden_ready")
        s_ht = sem("hidden_turned")
        s_hth = sem("ht_h_ready")
        s_htl = sem("ht_l_ready")
        s_yfree = sem("y_banks_read")
        s_comb_done = sem("experts_summed")
        s_most = sem("most_ready")
        s_accs = sem("acc_summed")
        s_done = sem("moe_done")
        s_fsq = sem("final_squares_ready")
        s_fstd = sem("final_std_ready")
        s_out = sem("out_ready")
        s_stored = sem("out_stored")
        s_link = sem("dve_chain")

        w_in = conv_w_in.rearrange("(c p) n -> p c n", p=P)
        w_out = conv_w_out.rearrange("(c p) n -> p c n", p=P)
        w_fg = ffn_gate.rearrange("(c p) n -> p c n", p=P)
        w_fu = ffn_up.rearrange("(c p) n -> p c n", p=P)
        w_fd = ffn_down.rearrange("(m c p) n -> p m c n", p=P, c=7)
        w_qkv_v = w_qkv.rearrange("(c p) n -> p c n", p=P)
        w_o_v = w_o.rearrange("(c p) n -> p c n", p=P)
        out_v = out.rearrange("a (t p) d -> p (a t) d", p=P)

        def load_expert_unit(sp, e, u, wait, place_of=None, landed=None):
            kind, fb, part = ORDER[u]
            slot = moe_slot(u)
            into = raw[:, slot, :] if place_of is None else place_of
            if wait is not None:
                if isinstance(wait, int) and wait < RING:
                    before = max(n for n in range(U_MOE) if n % DENSE_RING == slot)
                    sp.wait_ge(s_lo, 2 * before + 2)
                else:
                    sp.wait_ge(s_lo, 2 * (U_MOE + wait - RING) + 2)
            if kind == "down":
                src = moe_down[bass.ds(e * FF + 512 * fb + 256 * part, 256), :].rearrange("(c p) n -> p c n", p=P)
                dst = into.rearrange("p (c n) -> p c n", n=D)
            else:
                w = moe_gate if kind == "gate" else moe_up
                src = w[bass.ds(e * D + 512 * part, 512), 512 * fb:512 * (fb + 1)].rearrange(
                    "(c p) n -> p c n", p=P)
                dst = into.rearrange("p (c n) -> p c n", n=512)
            sp.dma_start(dst, src).then_inc(s_raw[slot] if landed is None else landed, 16)

        def overflow(eng, body):
            eng.wait_ge(s_most, 1)
            count = eng.value_load(most_i[0:1, 0:1], min_val=0, max_val=SEQ)
            with eng.If(count > P):
                body()

        block = ctx.enter_context(nc.Block())

        @block.sync
        def _(sp):
            x_v = x_t.rearrange("(c p) t -> p c t", p=P)

            def load(n, slot, src, wait=True, size=UNIT):
                if wait:
                    sp.wait_ge(s_lo, 2 * n - 2 * DENSE_RING + 2)
                dst = raw[:, slot, 0:size].rearrange("p (c n) -> p c n", n=256)
                sp.dma_start(dst, src).then_inc(s_raw[slot], 16)

            sp.dma_start(h[:, 0:4, :], x_v[:, 0:4, :]).then_inc(s_h[0], 16)
            sp.dma_start(params[:, 0:FIRST_PARAMS], params_d[:, 0:FIRST_PARAMS]).then_inc(s_first, 16)
            for m in range(N_IN):
                at = D * (2 - m // 4) + 256 * (m % 4)
                if m == 1:
                    sp.dma_start(h[:, 4:DC, :], x_v[:, 4:DC, :]).then_inc(s_h[1], 16)
                    sp.dma_start(consts[:, 0:FIRST_CONSTS], consts_d[:, 0:FIRST_CONSTS]).then_inc(s_ones, 16)
                load(U_IN + m, m % 4, w_in[:, :, at:at + 256], wait=m >= DENSE_RING)
            sp.dma_start(consts[:, FIRST_CONSTS:N_CONSTS], consts_d[:, FIRST_CONSTS:N_CONSTS]).then_inc(s_rest, 16)
            sp.dma_start(params[:, FIRST_PARAMS:N_PARAMS], params_d[:, FIRST_PARAMS:N_PARAMS]).then_inc(s_rest, 16)
            for k in range(RING - DENSE_RING):
                load_expert_unit(sp, 0, k, wait=None)
            for s in range(4):
                load(U_OUT + s, s, w_out[:, :, 256 * s:256 * (s + 1)])
            with sp.Fori(0, 7) as i:
                for s in range(4):
                    w = (w_fg, w_fu)[s % 2]
                    load(U_UP + 4 * i + s, s, w[:, :, bass.ds(512 * i + 256 * (s // 2), 256)])
            with sp.Fori(0, 4) as q:
                for s in range(4):
                    load(U_DOWN + 4 * q + s, s, w_fd[:, s, :, bass.ds(256 * q, 256)], size=7 * 256)
            for m in range(N_QKV):
                at = D + 256 * m if m < 2 else 256 * (m - 2)
                load(U_QKV + m, (U_QKV + m) % 4, w_qkv_v[:, :, at:at + 256])
            for m in range(N_O):
                load(U_O + m, (U_O + m) % 4, w_o_v[:, :, 256 * m:256 * (m + 1)])

            def experts(r):
                first = RING - DENSE_RING if r == 0 else 2
                for u in range(first, EXPERT_UNITS):
                    if r == 0 and u == RING - DENSE_RING + 2:
                        sp.wait_ge(s_used, 2 * (U_DOWN + N_DOWN))
                        for k in range(PARKED):
                            load_expert_unit(sp, 0, RING + k, None, parked[:, k, :], s_parked[k])
                    if r or not RING <= u < RING + PARKED:
                        load_expert_unit(sp, 0, u, wait=r * NE * EXPERT_UNITS + u)
                with sp.Fori(1, NE) as e:
                    for u in range(EXPERT_UNITS):
                        load_expert_unit(sp, e, u, wait=(r * NE + e) * EXPERT_UNITS + u)
                for u in range(2):
                    load_expert_unit(sp, 0, u, wait=(r + 1) * NE * EXPERT_UNITS + u)

            experts(0)
            overflow(sp, lambda: experts(1))
            for t in range(2):
                sp.wait_ge(s_out, t + 1)
                sp.dma_start(out_v[:, t, :], acc[:, t, :]).then_inc(s_stored, 16)
            sp.wait_ge(s_stored, 32)

        @block.scalar
        def _(act):
            def split_hi(n, slot, parity, fill):
                act.wait_ge(s_raw[slot], 16 * fill)
                for x in range(2):
                    if not (isinstance(n, int) and 2 * n + x < SPLITS):
                        act.wait_ge(s_used, 2 * n + x - SPLITS + 1)
                    nc.scalar.copy(hi[:, 2 * parity + x, :],
                                   raw[:, slot, HALF * x:HALF * (x + 1)]).then_inc(s_hi, 1)

            def dense_hi(n):
                slot, fill = dense_place(n)
                split_hi(n, slot, n % 2, fill)

            def stream_hi(name, c):
                nc.scalar.activation(xh[:, c, :], h[:, c, :], ACT.Copy, scale=param(name, c, 1)).then_inc(s_xh, 1)

            def stream_pair(name, q, tiles):
                for j in range(2):
                    act.wait_ge(s_tile_dve, tiles + j + 1)
                    stream_hi(name, 2 * q + j)
                nc.scalar.activation(sq[:, 2 * q:2 * q + 2, :], h[:, 2 * q:2 * q + 2, :], ACT.Square).then_inc(s_sq, 1)

            def std(k):
                act.wait_ge(s_ss, k + 1)
                nc.scalar.activation(rstd[:], bank[7][:, 0:L], ACT.Sqrt, bias=eps_col,
                                     scale=1.0 / D).then_inc(s_std, 1)

            eps_col = const("eps")
            act.sem_inc(s_tile_act, 4)
            act.sem_inc(s_silu, 2)
            act.sem_inc(s_yfree, 2)
            act.wait_ge(s_first, 16)
            for half in range(2):
                act.wait_ge(s_h[half], 16)
                for c in range(4 * half, 4 * half + 4):
                    stream_hi("conv_norm", c)
                if half == 0:
                    dense_hi(0)
            nc.scalar.activation(sq[:], h[:], ACT.Square).then_inc(s_sq, 4)
            dense_hi(1)
            act.wait_ge(s_ones, 16)
            std(0)

            for m in range(N_IN):
                n = U_IN + m
                if m >= 8:
                    for j in range(2):
                        blk = 2 * (m - 8) + j
                        act.wait_ge(s_tile_dve, 8 + 16 + blk + 1)
                        nc.scalar.copy(yh[:, blk, :], conv[:, blk, :]).then_inc(s_yh, 1)
                dense_hi(n + 2)
            for m in range(N_OUT):
                stream_pair("ffn_norm", m, 32 + 2 * m)
                dense_hi(U_OUT + m + 2)
            std(1)

            with act.Fori(0, 7) as i:
                for par in range(2):
                    p = 2 * i + par
                    gate_unit = U_UP + 4 * i + 2 * par
                    for j in range(2):
                        act.wait_ge(s_scaled, 2 * p + j + 1)
                        act.wait_ge(s_hid, 2 * p + j + 3)
                        nc.scalar.activation(gate_act[:, j, :], bank[4 * par + j][:, 0:L],
                                             ACT.Silu).then_inc(s_tile_act, 1)
                    for k in (2, 3):
                        ph = 2 * par + k
                        split_hi(gate_unit + k, ph % 4, ph % 2, U_UP // 4 + i + 1 + ph // 4)
                    for j in range(2):
                        act.wait_ge(s_hid, 4 + 2 * p + j + 1)
                        nc.scalar.copy(hid_h[:, bass.ds(2 * p + j, 1), :], hid[:, j:j + 1, :]).then_inc(s_hidh, 1)
            for m in range(N_DOWN):
                if m % 4 == 3:
                    stream_pair("attn_norm", m // 4, 40 + 2 * (m // 4))
                dense_hi(U_DOWN + m + 2)
            std(2)

            for m in range(N_QKV):
                n = U_QKV + m
                for j in range(2):
                    tile = 2 * m + j
                    act.wait_ge(s_scaled, N_UP + tile + 1)
                    src = bank[tile % 8]
                    if m < 2:
                        nc.scalar.activation(kv_t[:, tile, :], src[:, 0:L], ACT.Identity,
                                             bias=param("b_qkv", 8 + tile, 1)).then_inc(s_tile_act, 1)
                    else:
                        b = tile - 4
                        nc.scalar.activation(q_t[:, b, :], src[:, 0:SEQ], ACT.Identity,
                                             bias=param("b_qkv", b, 1)).then_inc(s_tile_act, 1)
                dense_hi(n + 2)
                for g in (2 * (m - 3), 2 * (m - 3) + 1) if m in (3, 4) else ():
                    act.wait_ge(s_krope, g + 1)
                    if g == 0:
                        act.wait_ge(s_kzero, 1)
                    for i in range(2):
                        half = slice(HD * i, HD * (i + 1))
                        nc.scalar.copy(k_rot[half, g, i, :], bank[2 + g][half, 0:L]).then_inc(s_krot, 1)
            act.wait_ge(s_v, 2)
            for i in range(2):
                nc.scalar.copy(v_meta[:, :, i, :],
                               bank[2][0:META, 0:256].rearrange("p (g d) -> p g d", d=HD)).then_inc(s_v_sb, 1)
                for t in range(2):
                    nc.scalar.copy(v_tok[:, t, :, i, :], bank[3][:, 256 * t:256 * (t + 1)].rearrange(
                        "p (g d) -> p g d", d=HD)).then_inc(s_v_sb, 1)

            def turned_probs(s):
                act.wait_ge(s_pt, s + 1)
                if s >= 2:
                    act.wait_ge(s_pv, s - 1)
                src = bank[4 + s % 2][:].rearrange("p (k i q) -> p k i q", k=2, i=2)
                dst = prob_t[:, s % 2]
                if s < 8:
                    nc.scalar.copy(dst[0:META, 0], src[0:META, 0]).then_inc(s_pt_sb, 1)
                    nc.scalar.copy(dst[:, 1], src[:, 1]).then_inc(s_pt_sb, 1)
                else:
                    nc.scalar.copy(dst, src).then_inc(s_pt_sb, 2)

            def output_hi(s):
                t, b = s // 8, s % 8
                act.wait_ge(s_pv, s + 1)
                for i in range(2):
                    half = slice(HD * i, HD * (i + 1))
                    nc.scalar.copy(oh[half, b, P * t:P * (t + 1)],
                                   bank[6 + s % 2][half, P * i:P * (i + 1)]).then_inc(s_oh, 1)

            for s in range(STEPS + 5):
                t, b = s // 8, s % 8
                k0 = P - META if t == 0 else 0
                if s >= 5:
                    output_hi(s - 5)
                if 3 <= s < STEPS + 3:
                    turned_probs(s - 3)
                if s >= STEPS:
                    continue
                act.wait_ge(s_negmax, s + 1)
                for i in range(2):
                    nc.scalar.activation(prob[:, s % PROBS, i, k0:], prob[:, s % PROBS, i, k0:], ACT.Exp,
                                         bias=neg_max[:, t, 2 * b + i:2 * b + i + 1],
                                         accum_out=prob_sum[:, t, 2 * b + i:2 * b + i + 1]).then_inc(s_exp, 1)

            def turned_stream(g):
                side, what, t = TURNS[g]
                act.wait_ge(s_turned, g + 1)
                nc.scalar.copy((acc, xt_h)[what][:, t, 512 * side:512 * (side + 1)],
                               bank[TURN_BANK[g]][:]).then_inc(s_turn_read, 1)

            for m in range(N_O):
                for j in range(2):
                    blk = 2 * m + j
                    act.wait_ge(s_tile_dve, 48 + blk + 1)
                    nc.scalar.activation(xg[:, blk, :], h[:, blk, META:L], ACT.Copy,
                                         scale=param("moe_norm", blk, 1)).then_inc(s_xg, 1)
                nc.scalar.activation(sq[:, 2 * m:2 * m + 2, META:L], h[:, 2 * m:2 * m + 2, META:L],
                                     ACT.Square).then_inc(s_sq, 1)
                dense_hi(U_O + m + 2)
                if m == 2:
                    for g in range(4):
                        turned_stream(g)
            for g in range(4, 8):
                turned_stream(g)
            act.wait_ge(s_tsq, 1)
            nc.scalar.activation(final_std[:], bank[6][:, 0:2], ACT.Sqrt, bias=eps_col,
                                 scale=1.0 / D).then_inc(s_tstd, 1)

            def turned_hi(e, fb):
                act.wait_ge(s_ht, FB * e + fb + 1)
                nc.scalar.copy(ht_h[:, fb % 2], bank[4][:].rearrange("p (c n) -> p c n", c=4)).then_inc(s_hth, 1)

            def gathered_slots(before, g):
                act.wait_ge(s_gath, before + g + 1)
                nc.scalar.copy(xs[:, 512 * g:512 * (g + 1)], bank[GATHER_BANK[g]][:]).then_inc(s_xs, 1)

            def gathered_hi(times, g):
                act.wait_ge(s_xst, 2 * times + g + 1)
                nc.scalar.copy(xe_h[:, 4 * g:4 * g + 4, :],
                               bank[SLOTS_BANK[g]][:].rearrange("p (c n) -> p c n", c=4)).then_inc(s_xeh, 1)

            def experts(r):
                for g in range(2):
                    gathered_slots(gathered(r), g)
                for g in range(2):
                    gathered_hi((NE + 1) * r, g)
                if r == 0:
                    act.wait_ge(s_top, 1)
                    for t in range(2):
                        nc.scalar.activation(combine[:, t, :], logit[:, t, :], ACT.Exp, bias=neg_top_r[:, t:t + 1],
                                             scale=tok_rstd[:, t:t + 1]).then_inc(s_gexp, 1)
                with act.Fori(0, NE) as el:
                    e = el + NE * r
                    use = USES * e
                    gath = GATHERS * (e + r + 1)
                    for u, (kind, fb, part) in enumerate(ORDER):
                        n = U_MOE + EXPERT_UNITS * e + u
                        if (kind, part) == ("gate", 1):
                            act.wait_ge(s_used, 2 * n + 2)
                            act.wait_ge(s_mult, FB * e + fb + (1 if fb else 2))
                            if fb == 0:
                                act.wait_ge(s_xe, gath)
                            nc.scalar.activation(silu_g[:, fb % 2, :], bank[fb % 2][:], ACT.Silu,
                                                 scale=slot_rstd[:]).then_inc(s_silu, 1)
                        if (kind, fb, part) == ("down", FB - 1, 1):
                            act.wait_ge(s_used, 2 * n + 2)
                            nc.scalar.copy(y[:, 0:512], bank[6][:]).then_inc(s_yfree, 1)
                        slot = moe_slot((u + 2) % EXPERT_UNITS)
                        fill = dense_fills(slot) + (EXPERT_UNITS // RING) * e + (u + 2) // RING + 1
                        split_hi(n + 2, slot, u % 2, fill)
                        if (kind, part) == ("gate", 1) and fb:
                            turned_hi(e, fb - 1)
                        if (kind, fb, part) == PLACE_AT:
                            act.wait_ge(s_fill5, use + 5)
                            nc.scalar.copy(place[:], bank[5][:, 0:SEQ]).then_inc(s_read5, 1)
                        if (kind, fb, part) == ("up", FB - 1, 1):
                            gathered_slots(gath, 0)
                            gathered_slots(gath, 1)
                        if (kind, fb, part) == ("down", FB - 2, 0):
                            turned_hi(e, FB - 1)
                        if (kind, fb, part) == ("down", FB - 2, 1):
                            gathered_hi(e + r + 1, 0)
                            gathered_hi(e + r + 1, 1)

            experts(0)
            overflow(act, lambda: experts(1))
            nc.scalar.activation(final_std[:, 0:1], eps_col, ACT.Sqrt).then_inc(s_fsq, 1)
            act.wait_ge(s_done, 1)
            for t in range(2):
                act.wait_ge(s_fsq, t + 1)
                nc.scalar.activation(squares[:], acc[:, t, :], ACT.Square,
                                     accum_out=sq_sum[:, t:t + 1]).then_inc(s_fsq, 1)
            act.wait_ge(s_fsq, 3)
            nc.scalar.activation(final_std[:], sq_sum[:], ACT.Sqrt, bias=eps_col, scale=1.0 / D).then_inc(s_fstd, 1)

        @block.vector
        def _(dve):
            v = nc.vector
            links = [0]

            def link(ins):
                links[0] += 1
                ins.then_inc(s_link, 1)
                dve.wait_ge(s_link, links[0])

            def split_lo(n, slot, parity):
                for x in range(2):
                    dve.wait_ge(s_hi, 2 * n + x + 1)
                    at = 2 * parity + x
                    v.tensor_tensor(lo[:, at, :], raw[:, slot, HALF * x:HALF * (x + 1)], hi[:, at, :].bitcast(F32),
                                    ALU.subtract).then_inc(s_lo, 1)

            def dense_lo(n):
                split_lo(n, dense_place(n)[0], n % 2)

            def stream_lo(k, name, c):
                dve.wait_ge(s_xh, DC * k + c + 1)
                v.scalar_tensor_tensor(out=xl[:, c, :], in0=h[:, c, :], scalar=param(name, c, 1),
                                       in1=xh[:, c, :].bitcast(F32), op0=ALU.mult,
                                       op1=ALU.subtract).then_inc(s_xl, 1)

            def sum_squares(k, t0=0):
                dve.wait_ge(s_sq, 4 * (k + 1))
                v.tensor_reduce(rstd[:, t0:L], sq[:, :, t0:L].rearrange("p c t -> p t c"), AX,
                                ALU.add).then_inc(s_sq_sum, 1)

            def invert_rms(k):
                dve.wait_ge(s_std, k + 1)
                link(v.reciprocal(rstd[:], rstd[:]))

            def scale_tiles(tiles, t0=0):
                for src in tiles:
                    v.tensor_tensor(src[:, 0:L - t0], src[:, 0:L - t0], rstd[:, t0:L], ALU.mult).then_inc(s_scaled, 1)

            dve.sem_inc(s_hid, 4)
            dve.sem_inc(s_hidl, 2)
            dve.sem_inc(s_mult, 2)
            dve.sem_inc(s_htl, 1)
            dve.sem_inc(s_read5, 1)
            v.memset(v_act[:, :, 0:2], 0.0).then_inc(s_tile_dve, 8)
            for half in range(2):
                for c in range(4 * half, 4 * half + 4):
                    stream_lo(0, "conv_norm", c)
                if half == 0:
                    dense_lo(0)
            sum_squares(0)
            dense_lo(1)
            invert_rms(0)
            link(v.tensor_tensor(rstd_sq[:], rstd[:], rstd[:], ALU.mult))

            for m in range(N_IN):
                n = U_IN + m
                dve.wait_ge(s_used, 2 * n + 2)
                for j in range(2):
                    tile = 2 * m + j
                    blk = tile % 8
                    src = bank[blk][:, 0:L]
                    if m < 4:
                        v.tensor_tensor(u_act[:, blk, :], src, rstd_sq[:], ALU.mult).then_inc(s_tile_dve, 1)
                    elif m < 8:
                        v.tensor_tensor(v_act[:, blk, 2:], src, u_act[:, blk, :], ALU.mult).then_inc(s_tile_dve, 1)
                    else:
                        v.tensor_tensor(conv[:, blk, :], src, conv[:, blk, :], ALU.mult).then_inc(s_tile_dve, 1)
                for blk in (2 * (m - 8), 2 * (m - 8) + 1) if m >= 8 else ():
                    dve.wait_ge(s_yh, blk + 1)
                    v.tensor_tensor(yl[:, blk, :], conv[:, blk, :], yh[:, blk, :].bitcast(F32),
                                    ALU.subtract).then_inc(s_yl, 1)
                dense_lo(n + 2)
                for j in range(2):
                    tile = 2 * m + j
                    blk = tile % 8
                    if 4 <= m < 8:
                        dve.wait_ge(s_tile_dve, 8 + tile + 1)
                        link(v.tensor_scalar(conv[:, blk, :], v_act[:, blk, 0:L], param("conv_w", blk, 1), None,
                                             ALU.mult))
                        for k in (1, 2):
                            link(v.scalar_tensor_tensor(out=conv[:, blk, :], in0=v_act[:, blk, k:k + L],
                                                        scalar=param("conv_w", DC * k + blk, 1),
                                                        in1=conv[:, blk, :], op0=ALU.mult, op1=ALU.add))

            def add_tile(tile, src, t0):
                v.tensor_tensor(h[:, tile, t0:L], h[:, tile, t0:L], src[:, 0:L - t0], ALU.add).then_inc(s_tile_dve, 1)

            def add_scaled(q, tiles):
                for src in tiles:
                    ins = v.tensor_tensor(src[:, 0:L], src[:, 0:L], rstd[:], ALU.mult)
                    if src is tiles[0]:
                        ins.then_inc(s_link, 1)
                        links[0] += 1
                link(ins)
                for j in range(2):
                    add_tile(2 * q + j, tiles[j], 0)

            for m in range(N_OUT):
                dve.wait_ge(s_used, 2 * (U_OUT + m) + 2)
                add_scaled(m, (bank[2 * m], bank[2 * m + 1]))
                for j in range(2):
                    stream_lo(1, "ffn_norm", 2 * m + j)
                if m == N_OUT - 1:
                    sum_squares(1)
                dense_lo(U_OUT + m + 2)
            invert_rms(1)

            with dve.Fori(0, 7) as i:
                for par in range(2):
                    p = 2 * i + par
                    gate_unit = U_UP + 4 * i + 2 * par
                    dve.wait_ge(s_used, 2 * gate_unit + 2)
                    scale_tiles((bank[4 * par], bank[4 * par + 1]))
                    split_lo(gate_unit + 2, (2 * par + 2) % 4, 0)
                    dve.wait_ge(s_used, 2 * gate_unit + 4)
                    for j in range(2):
                        dve.wait_ge(s_tile_act, 4 + 2 * p + j + 1)
                        dve.wait_ge(s_hidl, 2 * p + j + 1)
                        v.tensor_tensor(hid[:, j, :], bank[4 * par + 2 + j][:, 0:L], gate_act[:, j, :],
                                        ALU.mult).then_inc(s_hid, 1)
                    split_lo(gate_unit + 3, (2 * par + 3) % 4, 1)
                    for j in range(2):
                        dve.wait_ge(s_hidh, 2 * p + j + 1)
                        f = bass.ds(2 * p + j, 1)
                        v.tensor_tensor(hid_l[:, f, :], hid[:, j:j + 1, :], hid_h[:, f, :].bitcast(F32),
                                        ALU.subtract).then_inc(s_hidl, 1)

            for m in range(N_DOWN):
                if m % 4 == 3:
                    q = m // 4
                    dve.wait_ge(s_used, 2 * (U_DOWN + m) + 2)
                    add_scaled(q, (bank[2 * (q % 2)], bank[2 * (q % 2) + 1]))
                    for j in range(2):
                        stream_lo(2, "attn_norm", 2 * q + j)
                if m == N_DOWN - 1:
                    sum_squares(2)
                dense_lo(U_DOWN + m + 2)
            invert_rms(2)

            def rotate_q(b):
                if b == 0:
                    dve.wait_ge(s_rest, 32)
                if b >= 2:
                    dve.wait_ge(s_rot, b - 1)
                dve.wait_ge(s_rope, b + 1)
                v.tensor_tensor(q_sin[:, b % 2, :], bank[ROPE_BANK[b]][:, 0:SEQ], const("sin")[:, META:L],
                                ALU.mult).then_inc(s_rope_read, 1)
                dve.wait_ge(s_rope_read, b + 1)
                dve.wait_ge(s_qcos, b + 1)
                v.tensor_tensor(q_rot[:, b, :], q_rot[:, b, :], q_sin[:, b % 2, :], ALU.add).then_inc(s_rot, 1)

            for m in range(N_QKV):
                dve.wait_ge(s_used, 2 * (U_QKV + m) + 2)
                scale_tiles((bank[2 * m % 8], bank[2 * m % 8 + 1]), 0 if m < 2 else META)
                dense_lo(U_QKV + m + 2)
                if m == 4:
                    rotate_q(0)
                    rotate_q(1)
            dve.wait_ge(s_rest, 32)
            v.tensor_tensor(router_g[:], param("router").rearrange("p (c n) -> p c n", n=NE),
                            param("moe_norm").unsqueeze(2).to_broadcast([P, DC, NE]), ALU.mult).then_inc(s_router, 1)
            def part_of(s):
                return prob[:, s % PROBS, :, P - META if s < 8 else 0:]

            def mask_scores(s):
                k0 = P - META if s < 8 else 0
                width = 2 * P - k0
                dve.wait_ge(s_score, s + 1)
                if s >= PROBS:
                    dve.wait_ge(s_pt, s - PROBS + 1)
                mask = const("mask")[:, k0:].unsqueeze(1).to_broadcast([P, 2, width])
                scores = bank[2 + s % 2][:].rearrange("p (i k) -> p i k", i=2)[:, :, k0:]
                b = s % 8
                v.tensor_copy(part_of(s)[:, :, width], param("sinks", 2 * b, 2)).then_inc(s_masked, 1)
                v.scalar_tensor_tensor(out=part_of(s)[:, :, 0:width], in0=scores, scalar=HD ** -0.5, in1=mask, op0=ALU.mult,
                                       op1=ALU.add).then_inc(s_masked, 1)

            def find_max(s):
                t, b = s // 8, s % 8
                dve.wait_ge(s_masked, 2 * s + 2)
                if s:
                    dve.wait_ge(s_negmax, s)
                link(v.tensor_reduce(row_max[:], part_of(s), AX, ALU.max))
                v.tensor_scalar(neg_max[:, t, 2 * b:2 * b + 2], row_max[:], -1.0, None, ALU.mult).then_inc(s_negmax, 1)

            def inverse_sums(s):
                t, b = s // 8, s % 8
                heads = (slice(None), t, slice(2 * b, 2 * b + 2))
                dve.wait_ge(s_exp, 2 * (s + 1))
                link(v.reciprocal(prob_scale[heads], prob_sum[heads]))
                if s >= 2:
                    dve.wait_ge(s_pt, s - 1)
                v.tensor_tensor(inverse[:, s % 2], ident.unsqueeze(1).to_broadcast([P, 2, P]),
                                prob_scale[heads].unsqueeze(2).to_broadcast([P, 2, P]), ALU.mult).then_inc(s_inverse, 1)

            def output_lo(s):
                t, b = s // 8, s % 8
                for i in range(2):
                    dve.wait_ge(s_oh, 2 * s + i + 1)
                    half = slice(HD * i, HD * (i + 1))
                    dst = (half, b, slice(P * t, P * (t + 1)))
                    v.tensor_tensor(ol[dst], bank[6 + s % 2][half, P * i:P * (i + 1)], oh[dst].bitcast(F32),
                                    ALU.subtract).then_inc(s_ol, 1)

            rotate_q(2)
            for s in range(STEPS + 5):
                if s + 3 < DC:
                    rotate_q(s + 3)
                if s < STEPS:
                    mask_scores(s)
                if 1 <= s < STEPS + 1:
                    find_max(s - 1)
                if 2 <= s < STEPS + 2:
                    inverse_sums(s - 2)
                if s >= 5:
                    output_lo(s - 5)
            def turned_lo_stream(g):
                side, what, t = TURNS[g]
                dve.wait_ge(s_turn_read, g + 1)
                part = (slice(None), t, slice(512 * side, 512 * (side + 1)))
                v.tensor_tensor(xt_l[part], bank[TURN_BANK[g]][:], xt_h[part].bitcast(F32),
                                ALU.subtract).then_inc(s_xtl, 1)

            for m in range(N_O):
                dve.wait_ge(s_used, 2 * (U_O + m) + 2)
                for j in range(2):
                    add_tile(2 * m + j, bank[2 * m + j], META)
                dense_lo(U_O + m + 2)
                if m == 2:
                    turned_lo_stream(2)
                    turned_lo_stream(3)

            def gathered_lo(times, g):
                dve.wait_ge(s_xeh, 2 * times + g + 1)
                part = (slice(None), slice(4 * g, 4 * g + 4))
                v.tensor_tensor(xe_l[part], bank[SLOTS_BANK[g]][:].rearrange("p (c n) -> p c n", c=4),
                                xe_h[part].bitcast(F32), ALU.subtract).then_inc(s_xe, 1)

            def slot_scale(times):
                dve.wait_ge(s_gath, GATHERS * (times + 1))
                v.tensor_copy(slot_rstd[:], bank[GATHER_BANK[2]][:, 0:1]).then_inc(s_xe, 1)

            dve.wait_ge(s_logit, 1)
            link(v.tensor_copy(logit[:].rearrange("p t n -> p (t n)"), bank[6][:, 0:2 * NE]))
            other = logit[:].unsqueeze(2).to_broadcast([P, 2, NE, NE])
            own = logit[:].unsqueeze(3).to_broadcast([P, 2, NE, NE])
            earlier = const("earlier").rearrange("p (a b) -> p a b", a=NE).unsqueeze(1).to_broadcast([P, 2, NE, NE])
            link(v.tensor_tensor(pair_b[:], other, own, ALU.is_equal))
            link(v.tensor_tensor(pair_a[:], other, own, ALU.is_gt))
            link(v.tensor_tensor(pair_b[:], pair_b[:], earlier, ALU.mult))
            link(v.tensor_tensor(pair_a[:], pair_a[:], pair_b[:], ALU.add))
            link(v.tensor_reduce(rank[:], pair_a[:], AX, ALU.add))
            link(v.memset(route[:, NE, :], 0.0))
            by_tile = route[:, 0:NE, :].rearrange("p e (k t) -> p k t e", k=2)
            v.tensor_scalar(by_tile[:, 1], rank[:], 1.5, None, ALU.is_lt).then_inc(s_chosen, 1)
            link(v.tensor_scalar(chosen[:], rank[:], 1.5, None, ALU.is_lt))
            v.tensor_tensor(chosen_sum[:], chosen[:, 0], chosen[:, 1], ALU.add).then_inc(s_chosen, 1)
            turned_lo_stream(4)
            turned_lo_stream(5)
            sum_squares(3, META)
            dve.wait_ge(s_pos, 1)
            v.tensor_copy(by_tile[:, 0], bank[7][:, 0:2 * NE].rearrange("p (t e) -> p t e", t=2)).then_inc(s_slot, 1)
            link(v.tensor_reduce(most[:], bank[7][:, 2 * NE:3 * NE], AX, ALU.max))
            v.tensor_copy(most_i[:], most[:]).then_inc(s_most, 1)
            dve.wait_ge(s_tstd, 1)
            link(v.reciprocal(tok_rstd[:], final_std[:]))
            link(v.tensor_reduce(top[:], logit[:], AX, ALU.max))
            v.scalar_tensor_tensor(out=neg_top_r[:], in0=top[:], scalar=-1.0, in1=tok_rstd[:], op0=ALU.mult,
                                   op1=ALU.mult).then_inc(s_top, 1)
            for g in range(2):
                gathered_lo(0, g)
            slot_scale(0)
            dve.wait_ge(s_gexp, 2)
            link(v.tensor_tensor(combine[:], combine[:], chosen[:], ALU.mult))
            link(v.tensor_reduce(gate_sum[:], combine[:], AX, ALU.add))
            link(v.reciprocal(gate_sum[:], gate_sum[:]))
            v.tensor_tensor(gates[:].rearrange("p e t -> p t e"), combine[:],
                            gate_sum[:].unsqueeze(2).to_broadcast([P, 2, NE]), ALU.mult).then_inc(s_comb, 1)

            def turned_lo(e, fb):
                dve.wait_ge(s_hth, FB * e + fb + 1)
                v.tensor_tensor(ht_l[:, fb % 2], bank[4][:].rearrange("p (c n) -> p c n", c=4),
                                ht_h[:, fb % 2].bitcast(F32), ALU.subtract).then_inc(s_htl, 1)

            def experts(r):
                if r:
                    v.tensor_scalar(route[:, 0:NE, 0:2], route[:, 0:NE, 0:2], -float(P), None,
                                    ALU.add).then_inc(s_slot, 1)
                    for g in range(2):
                        gathered_lo((NE + 1) * r, g)
                    slot_scale((NE + 1) * r)
                with dve.Fori(0, NE) as el:
                    e = el + NE * r
                    use = USES * e
                    for u, (kind, fb, part) in enumerate(ORDER):
                        n = U_MOE + EXPERT_UNITS * e + u
                        if (kind, part) == ("up", 1):
                            dve.wait_ge(s_used, 2 * n + 2)
                            dve.wait_ge(s_silu, 2 + FB * e + fb + 1)
                            v.scalar_tensor_tensor(out=hid_e[:, fb % 2, :], in0=bank[2 + fb % 2][:],
                                                   scalar=slot_rstd[:], in1=silu_g[:, fb % 2, :], op0=ALU.mult,
                                                   op1=ALU.mult).then_inc(s_mult, 1)
                        if (kind, fb, part) == ("down", FB - 1, 1):
                            dve.wait_ge(s_used, 2 * n + 2)
                            v.tensor_copy(y[:, 512:D], bank[7][:]).then_inc(s_yfree, 1)
                        split_lo(n + 2, moe_slot((u + 2) % EXPERT_UNITS), u % 2)
                        if (kind, part) == ("gate", 1) and fb:
                            turned_lo(e, fb - 1)
                        if (kind, fb, part) in COMBINE_AT:
                            g = COMBINE_AT.index((kind, fb, part))
                            dve.wait_ge(s_fill5, use + g + 1)
                            acc_part = acc[:, g // 2, 512 * (g % 2):512 * (g % 2 + 1)]
                            v.tensor_tensor(acc_part, acc_part, bank[5][:], ALU.add).then_inc(s_read5, 1)
                        if (kind, fb, part) == ("down", FB - 2, 0):
                            turned_lo(e, FB - 1)
                            slot_scale(e + r + 1)
                        if (kind, fb, part) == ("down", FB - 2, 1):
                            gathered_lo(e + r + 1, 0)
                            gathered_lo(e + r + 1, 1)
                for g in range(4):
                    dve.wait_ge(s_comb_done, 4 * r + g + 1)
                    acc_part = acc[:, g // 2, 512 * (g % 2):512 * (g % 2 + 1)]
                    v.tensor_tensor(acc_part, acc_part, bank[g][:], ALU.add).then_inc(s_accs, 1)
                dve.wait_ge(s_accs, 4 * (r + 1))

            experts(0)
            overflow(dve, lambda: experts(1))
            dve.sem_inc(s_done, 1)
            dve.wait_ge(s_fstd, 1)
            v.reciprocal(final_rstd[:], final_std[:]).then_inc(s_done, 1)
            dve.wait_ge(s_done, 2)
            for t in range(2):
                v.scalar_tensor_tensor(out=acc[:, t, :], in0=acc[:, t, :], scalar=final_rstd[:, t:t + 1],
                                       in1=param("final_norm"), op0=ALU.mult, op1=ALU.mult).then_inc(s_out, 1)

        @block.gpsimd
        def _(pool):
            g = nc.gpsimd
            cos, sin = const("cos"), const("sin")
            pool.wait_ge(s_rest, 32)
            pool.wait_ge(s_used, 2 * (U_DOWN + N_DOWN))
            g.memset(k_rot[:], 0.0).then_inc(s_kzero, 1)
            for c in range(2):
                pool.wait_ge(s_tile_act, 4 + N_UP + c + 1)
                g.tensor_tensor(k_cos[:, c, :], kv_t[:, c, :], cos, ALU.mult).then_inc(s_kcs, 1)
                g.tensor_tensor(k_sin[:, c, :], kv_t[:, c, :], sin, ALU.mult).then_inc(s_kcs, 1)
            for b in range(DC):
                pool.wait_ge(s_tile_act, 4 + N_UP + 4 + b + 1)
                g.tensor_tensor(q_rot[:, b, :], q_t[:, b, :], cos[:, META:L], ALU.mult).then_inc(s_qcos, 1)

            def pick_tokens(e):
                for t in range(2):
                    g.tensor_scalar(pick[:, t, :], const("iota"), route[:, e, t:t + 1], route[:, e, 2 + t:3 + t],
                                    ALU.is_equal, ALU.mult).then_inc(s_pick, 1)

            def experts(r):
                pool.wait_ge(s_slot, r + 1)
                pool.wait_ge(s_chosen, 2)
                if r:
                    pool.wait_ge(s_comb_done, 4)
                pick_tokens(0)
                pool.wait_ge(s_turned, 8)
                pool.wait_ge(s_tsq, 1)
                g.memset(y[:], 0.0).then_inc(s_zero, 1)
                g.memset(place[:], 0.0).then_inc(s_zero, 1)
                for k in range(PARKED) if r == 0 else ():
                    pool.wait_ge(s_parked[k], 16)
                    pool.wait_ge(s_lo, 2 * (U_MOE + k) + 2)
                    slot = moe_slot(k)
                    g.tensor_copy(raw[:, slot, :], parked[:, k, :]).then_inc(s_raw[slot], 16)
                pool.wait_ge(s_comb, 1)
                for e in range(NE):
                    pool.wait_ge(s_gath, gathered(r) + GATHERS * (e + 1))
                    for t in range(2):
                        g.tensor_scalar(placed[:, t, :], const("iota"), route[:, e, t:t + 1], gates[:, e, t:t + 1],
                                        ALU.is_equal, ALU.mult).then_inc(s_placed, 1)
                    pick_tokens(e + 1)

            experts(0)
            overflow(pool, lambda: experts(1))

        @block.tensor
        def _(pe):
            mm = nc.tensor.matmul

            def dense_unit(n, parity, banks, width, moving, chunks, first, last, ready_in=None):
                for x in range(2):
                    if ready_in is not None:
                        pe.wait_ge(ready_in[0], ready_in[1 + x])
                    at = 2 * parity + x
                    todo = [c for c in chunks if c // 4 == x]
                    for part, ready in ((hi, s_hi), (lo, s_lo)):
                        pe.wait_ge(ready, 2 * n + x + 1)
                        for j in range(2):
                            dst = bank[banks[j]][:, 0:width]
                            for c in todo:
                                w = part[:, at, 256 * (c % 4) + P * j:256 * (c % 4) + P * (j + 1)]
                                begin = first and part is hi and c == 0
                                end = last and part is lo and c == chunks[-1]
                                ins = mm(dst, w, moving(0, c), start=begin, stop=end)
                                if part is hi:
                                    ins = mm(dst, w, moving(1, c), start=False, stop=False)
                    ins.then_inc(s_used, 1)

            def stream(t0=0):
                return lambda part, c: (xh, xl)[part][:, c, t0:L]

            def square_sums(k):
                pe.wait_ge(s_sq_sum, k + 1)
                mm(bank[7][:, 0:L], const("ones"), rstd[:], start=True, stop=True).then_inc(s_ss, 1)

            every = list(range(DC))

            def conv_units(i):
                for s in range(4):
                    first = isinstance(i, int) and s == 0
                    pe.wait_ge(s_tile_dve, 8 * i + 2 * s + 2)
                    if isinstance(i, int) and s == 3:
                        pe.wait_ge(s_std, 1)
                    dense_unit(U_IN + 4 * i + s, s % 2, (2 * s, 2 * s + 1), L, stream(), every, True, True,
                               (s_xl, 4, 8) if first else None)
                    if first:
                        pe.wait_ge(s_ones, 16)
                        square_sums(0)

            conv_units(0)
            with pe.Fori(1, 3) as i:
                conv_units(i)
            for m in range(N_OUT):
                pe.wait_ge(s_tile_dve, 24 + 2 * m + 2)
                dense_unit(U_OUT + m, m % 2, (2 * m, 2 * m + 1), L, lambda part, c: (yh, yl)[part][:, c, :],
                           every, True, True, (s_yl, 4, 8) if m == 0 else None)

            def up_units(i):
                for s in range(4):
                    first = isinstance(i, int) and s == 0
                    p = 2 * i + s // 2
                    pe.wait_ge((s_tile_act, s_hid)[s % 2], 2 * p + 2)
                    if isinstance(i, int) and s == 3:
                        pe.wait_ge(s_std, 2)
                    dense_unit(U_UP + 4 * i + s, s % 2, (2 * s, 2 * s + 1), L, stream(), every, True, True,
                               (s_xl, DC + 4, DC + 8) if first else None)
                    if first:
                        square_sums(1)

            up_units(0)
            with pe.Fori(1, 7) as i:
                up_units(i)
            pe.wait_ge(s_hid, 4 + 2 * 13)
            with pe.Fori(0, 2) as qq:
                for q in range(2):
                    pe.wait_ge(s_tile_dve, 38 + 4 * qq + 2 * q)
                    for m in range(4):
                        pe.wait_ge(s_hidl, 2 + 7 * m + 7)
                        dense_unit(U_DOWN + 8 * qq + 4 * q + m, m % 2, (2 * q, 2 * q + 1), L,
                                   lambda part, c, m=m: (hid_h, hid_l)[part][:, 7 * m + c, :],
                                   list(range(7)), m == 0, m == 3)
            def rotate_k(g):
                pe.wait_ge(s_kcs, 2 * (g // 2) + 2)
                mm(bank[2 + g][:, 0:L], const(f"k_dup{g % 2}"), k_cos[:, g // 2, :], start=True, stop=False)
                mm(bank[2 + g][:, 0:L], const(f"k_swap{g % 2}"), k_sin[:, g // 2, :], start=False,
                   stop=True).then_inc(s_krope, 1)

            def turn_q(b):
                mm(bank[ROPE_BANK[b]][:, 0:SEQ], const("q_swap"), q_t[:, b, :], start=True, stop=True).then_inc(s_rope, 1)

            for m in range(N_QKV):
                if m == 3:
                    pe.wait_ge(s_std, 3)
                if m == 5:
                    pe.wait_ge(s_krot, 4)
                if m >= 4:
                    pe.wait_ge(s_tile_act, 32 + 2 * (m - 4) + 2)
                t0 = 0 if m < 2 else META
                dense_unit(U_QKV + m, m % 2, (2 * m % 8, 2 * m % 8 + 1), L - t0, stream(t0), every, True, True,
                           (s_xl, 2 * DC + 4, 2 * DC + 8) if m == 0 else None)
                if m == 0:
                    square_sums(2)
                if m == 3:
                    pe.wait_ge(s_rest, 32)
                    rotate_k(0)
                    rotate_k(1)
                if m == 4:
                    pe.wait_ge(s_tile_act, 40)
                    rotate_k(2)
                    rotate_k(3)
                    turn_q(0)
                    turn_q(1)

            pe.wait_ge(s_krot, 8)
            turn_q(2)
            turn_q(3)
            pe.wait_ge(s_tile_act, 44)
            for b in (4, 5):
                pe.wait_ge(s_rope_read, b - 3)
                turn_q(b)
            for c in range(2):
                ins = nc.tensor.transpose(bank[2][0:META, P * c:P * (c + 1)], kv_t[:, 2 + c, 0:META], ident)
            ins.then_inc(s_v, 1)
            for t in range(2):
                for c in range(2):
                    at = 2 * P * t + P * c
                    ins = nc.tensor.transpose(bank[3][:, at:at + P], kv_t[:, 2 + c, META + P * t:META + P * (t + 1)],
                                              ident)
            ins.then_inc(s_v, 1)

            turn_q(6)
            turn_q(7)
            pe.wait_ge(s_v_sb, 6)

            def scores(s):
                t, b = s // 8, s % 8
                k0, k1 = ((0, META + P), (META, L))[t]
                if s < 8:
                    pe.wait_ge(s_rot, b + 1)
                if s >= 2:
                    pe.wait_ge(s_masked, 2 * (s - 1))
                for i in range(2):
                    dst = bank[2 + s % 2][:, 2 * P * (i + 1) - (k1 - k0):2 * P * (i + 1)]
                    ins = mm(dst, q_rot[:, b, P * t:P * (t + 1)], k_rot[:, b // 2, i, k0:k1], start=True, stop=True)
                ins.then_inc(s_score, 1)

            def turn_probs(s):
                pe.wait_ge(s_inverse, s + 1)
                if s >= 2:
                    pe.wait_ge(s_pt_sb, 2 * (s - 1))
                dst = bank[4 + s % 2][:].rearrange("p (k i q) -> p k i q", k=2, i=2)
                for i in range(2):
                    for k in range(2):
                        n = META if s < 8 and k == 0 else P
                        ins = mm(dst[0:n, k, i, :], prob[:, s % PROBS, i, P * (k + 1) - n:P * (k + 1)],
                                 inverse[:, s % 2, i, :], start=True, stop=True)
                ins.then_inc(s_pt, 1)

            def sum_values(s):
                t, b = s // 8, s % 8
                pe.wait_ge(s_pt_sb, 2 * (s + 1))
                if s >= 2:
                    pe.wait_ge(s_ol, 2 * (s - 1))
                g = b // 2
                values = ((v_meta[:, g], v_tok[:, 0, g]), (v_tok[:, 0, g], v_tok[:, 1, g]))[t]
                for k in range(2):
                    n = META if t == 0 and k == 0 else P
                    ins = mm(bank[6 + s % 2][:, 0:2 * P], values[k].rearrange("p i d -> p (i d)"),
                             prob_t[0:n, s % 2, k].rearrange("p i q -> p (i q)"), start=(k == 0), stop=(k == 1))
                ins.then_inc(s_pv, 1)

            for s in range(STEPS + 4):
                if s < STEPS:
                    scores(s)
                if 3 <= s < STEPS + 3:
                    turn_probs(s - 3)
                if s >= 4:
                    sum_values(s - 4)

            def turn_stream(g):
                side, what, t = TURNS[g]
                at = (META, 0)[what] + P * t
                for c in range(4):
                    src = (h, xg)[what][:, 4 * side + c, at:at + P]
                    ins = nc.tensor.transpose(bank[TURN_BANK[g]][:, P * c:P * (c + 1)], src, ident)
                ins.then_inc(s_turned, 1)

            for m in range(N_O):
                dense_unit(U_O + m, m % 2, (2 * m, 2 * m + 1), SEQ, lambda part, c: (oh, ol)[part][:, c, :],
                           every, True, True, (s_ol, 24, 32) if m == 0 else None)
                if m == 2:
                    pe.wait_ge(s_xg, 4)
                    for g in range(4):
                        turn_stream(g)
            pe.wait_ge(s_tile_dve, 56)
            pe.wait_ge(s_router, 1)
            for t in range(2):
                for c in range(DC):
                    at = META + P * t
                    ins = mm(bank[6][:, NE * t:NE * (t + 1)], h[:, c, at:at + P], router_g[:, c, :],
                             start=(c == 0), stop=(c == DC - 1))
            ins.then_inc(s_logit, 1)
            pe.wait_ge(s_xg, DC)
            for g in range(4, 6):
                turn_stream(g)
            pe.wait_ge(s_chosen, 2)
            mm(bank[7][:, 0:NE], const("before"), chosen[:, 0, :], start=True, stop=True)
            mm(bank[7][:, NE:2 * NE], const("ones"), chosen[:, 0, :], start=True, stop=False)
            mm(bank[7][:, NE:2 * NE], const("before"), chosen[:, 1, :], start=False, stop=True)
            mm(bank[7][:, 2 * NE:3 * NE], const("ones"), chosen_sum[:], start=True, stop=True).then_inc(s_pos, 1)
            for g in range(6, 8):
                pe.wait_ge(s_turn_read, g - 5)
                turn_stream(g)
            pe.wait_ge(s_sq_sum, 4)
            for t in range(2):
                at = META + P * t
                ins = mm(bank[6][:, t:t + 1], rstd[:, at:at + P], const("ones")[:, 0:1], start=True,
                         stop=True)
            ins.then_inc(s_tsq, 1)

            def gather(g):
                for t in range(2):
                    for src in (xt_h, xt_l):
                        ins = mm(bank[GATHER_BANK[g]][:], pick[:, t, :], src[:, t, 512 * g:512 * (g + 1)],
                                 start=(t == 0 and src is xt_h), stop=(t == 1 and src is xt_l))
                ins.then_inc(s_gath, 1)

            def turn_slots(times, g):
                pe.wait_ge(s_xs, 2 * times + g + 1)
                for c in range(4):
                    at = 512 * g + P * c
                    ins = nc.tensor.transpose(bank[SLOTS_BANK[g]][:, P * c:P * (c + 1)], xs[:, at:at + P], ident)
                ins.then_inc(s_xst, 1)

            def slot_scales():
                for t in range(2):
                    ins = mm(bank[GATHER_BANK[2]][:, 0:1], pick[:, t, :].bitcast(F32), tok_rstd[:, t:t + 1],
                             start=(t == 0), stop=(t == 1))
                ins.then_inc(s_gath, 1)

            def combine_experts(dst, g, done):
                t, side = g // 2, g % 2
                mm(dst, place[:, P * t:P * (t + 1)], y[:, 512 * side:512 * (side + 1)], start=True,
                   stop=True).then_inc(done, 1)

            def experts(r):
                if r == 0:
                    pe.wait_ge(s_turn_read, 8)
                else:
                    pe.wait_ge(s_accs, 4)
                pe.wait_ge(s_pick, 2 * (NE + 1) * r + 2)
                if r == 0:
                    pe.wait_ge(s_xtl, 4)
                for g in range(2):
                    gather(g)
                for g in range(2):
                    turn_slots((NE + 1) * r, g)
                pe.wait_ge(s_top, 1)
                slot_scales()
                if r == 0:
                    pe.wait_ge(s_most, 1)
                pe.wait_ge(s_zero, 2 * (r + 1))

                with pe.Fori(0, NE) as el:
                    e = el + NE * r
                    use = USES * e

                    def turn_hidden(fb):
                        pe.wait_ge(s_mult, 2 + FB * e + fb + 1)
                        pe.wait_ge(s_htl, FB * e + fb + 1)
                        for c in range(4):
                            ins = nc.tensor.transpose(bank[4][:, P * c:P * (c + 1)],
                                                      hid_e[:, fb % 2, P * c:P * (c + 1)], ident)
                        ins.then_inc(s_ht, 1)

                    for u, (kind, fb, part) in enumerate(ORDER):
                        n = U_MOE + EXPERT_UNITS * e + u
                        if part == 0 and kind == "gate":
                            if fb == 0:
                                pe.wait_ge(s_xe, GATHERS * (e + r + 1))
                            pe.wait_ge(s_silu, FB * e + fb + (1 if fb else 2))
                        if part == 0 and kind == "up":
                            pe.wait_ge(s_mult, FB * e + fb + (1 if fb else 2))
                        if part == 0 and kind == "down":
                            pe.wait_ge(s_htl, 1 + FB * e + fb + 1)
                            if fb == 0:
                                pe.wait_ge(s_yfree, 2 * e + 2)
                        for x in range(2):
                            at = 2 * (u % 2) + x
                            if kind == "down":
                                c = 2 * part + x
                                for w, ready in ((hi, s_hi), (lo, s_lo)):
                                    pe.wait_ge(ready, 2 * n + x + 1)
                                    for side in range(2):
                                        rhs = w[:, at, 512 * side:512 * (side + 1)]
                                        begin = fb == 0 and c == 0 and w is hi
                                        end = fb == FB - 1 and c == 3 and w is lo
                                        ins = mm(bank[6 + side][:], ht_h[:, fb % 2, c, :], rhs, start=begin, stop=end)
                                        if w is hi:
                                            mm(bank[6 + side][:], ht_l[:, fb % 2, c, :], rhs, start=False, stop=False)
                            else:
                                dst = bank[(0 if kind == "gate" else 2) + fb % 2][:]
                                for w, ready in ((hi, s_hi), (lo, s_lo)):
                                    pe.wait_ge(ready, 2 * n + x + 1)
                                    for k in range(2):
                                        c = 4 * part + 2 * x + k
                                        rhs = w[:, at, 512 * k:512 * (k + 1)]
                                        ins = mm(dst, xe_h[:, c, :], rhs, start=(c == 0 and w is hi),
                                                 stop=(c == DC - 1 and w is lo))
                                        if w is hi:
                                            mm(dst, xe_l[:, c, :], rhs, start=False, stop=False)
                            ins.then_inc(s_used, 1)
                        if (kind, part) == ("gate", 1) and fb:
                            turn_hidden(fb - 1)
                        if (kind, fb, part) in COMBINE_AT:
                            g = COMBINE_AT.index((kind, fb, part))
                            pe.wait_ge(s_yfree, 2 * e + 2)
                            pe.wait_ge(s_read5, use + g + 1)
                            combine_experts(bank[5][:], g, s_fill5)
                        if (kind, fb, part) == PLACE_AT:
                            pe.wait_ge(s_placed, 2 * e + 2)
                            pe.wait_ge(s_read5, use + 5)
                            for t in range(2):
                                ins = nc.tensor.transpose(bank[5][:, P * t:P * (t + 1)], placed[:, t, :], ident)
                            ins.then_inc(s_fill5, 1)
                        if (kind, fb, part) == ("up", FB - 1, 1):
                            pe.wait_ge(s_pick, 2 * e + 2 * r + 4)
                            pe.wait_ge(s_read5, use + 6)
                            for g in range(2):
                                gather(g)
                            slot_scales()
                        if (kind, fb, part) == ("down", FB - 2, 0):
                            turn_hidden(FB - 1)
                            for g in range(2):
                                turn_slots(e + r + 1, g)

                pe.wait_ge(s_yfree, 2 + 2 * NE * (r + 1))
                for g in range(4):
                    combine_experts(bank[g][:], g, s_comb_done)

            experts(0)
            overflow(pe, lambda: experts(1))


def constants():
    import numpy as np

    c = np.zeros((P, N_CONSTS), np.float32)

    def part(name):
        at, n = CONSTS[name]
        return c[:, at:at + n]

    row = np.arange(P)
    part("ident")[:] = np.eye(P)
    partner = (row + HD // 2) % HD
    sign = np.where(row % HD < HD // 2, -1.0, 1.0)
    part("q_swap")[HD * (row // HD) + partner, row] = sign
    for i in range(2):
        part(f"k_dup{i}")[HD * i + row % HD, row] = 1.0
        part(f"k_swap{i}")[HD * i + partner, row] = sign
    part("before")[:] = row[:, None] < row[None, :]
    part("ones")[:] = 1.0
    part("iota")[:] = row[None, :]
    back = P + row[:, None] - np.arange(2 * P)[None, :]
    part("mask")[:] = np.where((back >= 0) & (back < WINDOW), 0.0, MASKED)
    freq = (np.float32(10000.0) ** (-np.arange(0, HD, 2, dtype=np.float32) / np.float32(HD))).astype(np.float32)
    angle = np.arange(L, dtype=np.float32)[None, :] * freq[row % (HD // 2)][:, None]
    part("cos")[:] = np.cos(angle)
    part("sin")[:] = np.sin(angle)
    own, other = np.divmod(np.arange(NE * NE), NE)
    part("earlier")[:] = (other < own)[None, :]
    part("eps")[:] = EPS
    return c


def kernel(x, meta_tokens, conv_norm, conv_w_in, conv_w, conv_w_out, ffn_norm, ffn_w_gate, ffn_w_up,
           ffn_w_down, attn_norm, attn_w_qkv, attn_b_qkv, attn_sinks, attn_w_o, moe_norm, moe_w_router,
           moe_w_gate, moe_w_up, moe_w_down, final_norm):
    import numpy as np
    import concourse.bacc as bacc
    from concourse.bass_utils import run_bass_kernel_spmd

    def columns(a):
        return np.asarray(a).reshape(-1, P).T

    x_t = np.ascontiguousarray(np.concatenate([np.asarray(meta_tokens), np.asarray(x)[0]], axis=0).T)
    params = np.concatenate([
        columns(conv_norm), columns(ffn_norm), columns(attn_norm), columns(moe_norm),
        columns(conv_w), columns(attn_b_qkv),
        np.broadcast_to(np.asarray(attn_sinks).reshape(1, NH), (P, NH)),
        np.asarray(moe_w_router).reshape(DC, P, NE).transpose(1, 0, 2).reshape(P, DC * NE),
        np.broadcast_to(np.asarray(final_norm).reshape(1, D), (P, D)),
    ], axis=1)
    arrays = {
        "x_t": x_t, "consts_d": constants(), "params_d": np.ascontiguousarray(params),
        "conv_w_in": np.asarray(conv_w_in)[0], "conv_w_out": np.asarray(conv_w_out)[0],
        "ffn_gate": np.asarray(ffn_w_gate)[0], "ffn_up": np.asarray(ffn_w_up)[0],
        "ffn_down": np.asarray(ffn_w_down)[0], "w_qkv": np.asarray(attn_w_qkv)[0], "w_o": np.asarray(attn_w_o)[0],
        "moe_gate": np.asarray(moe_w_gate).reshape(NE * D, FF), "moe_up": np.asarray(moe_w_up).reshape(NE * D, FF),
        "moe_down": np.asarray(moe_w_down).reshape(NE * FF, D),
    }
    arrays = {name: np.ascontiguousarray(a) for name, a in arrays.items()}
    nc = bacc.Bacc("TRN2", target_bir_lowering=False, num_devices=1)
    ins = {name: nc.dram_tensor(f"in_{name}", a.shape, mybir.dt.from_np(a.dtype), kind="ExternalInput").ap()
           for name, a in arrays.items()}
    out = nc.dram_tensor("out_dram", (1, SEQ, D), F32, kind="ExternalOutput").ap()
    trunk(nc, **ins, out=out)
    result = run_bass_kernel_spmd(nc, [{f"in_{name}": a for name, a in arrays.items()}], core_ids=[0])
    return result.results[0]["out_dram"]
```
